# Optimizing a Trainium2 kernel written in Bass

```python
import jax, jax.numpy as jnp
from jax import lax
import numpy as np

D_MODEL = 1024
BATCH = 1
SEQ = 256
DEPTH = 2

CHUNK = 64
N_POOL_GROUPS = 4
POOL_WINDOWS = (2, 4, 8, 16)
POOL_GROUP_DIM = D_MODEL // N_POOL_GROUPS
HEAD_DIM = 64
N_Q_HEADS = D_MODEL // HEAD_DIM
N_KV_HEADS = 2
Q_PER_KV = N_Q_HEADS // N_KV_HEADS
WINDOW = 128
WINDOW_CHUNKS = WINDOW // CHUNK
ROPE_THETA = 10000.0
D_FF = 7 * D_MODEL // 2
N_EXPERTS = 8
TOP_K = 2
RMS_EPS = 1e-5
N_A_LAYERS = DEPTH // 2
N_B_LAYERS = DEPTH - N_A_LAYERS
N_DENSE_LAYERS = (DEPTH + 1) // 2
N_MOE_LAYERS = DEPTH // 2

kernel_name = "yoco_pool_swa_sink_moe_trunk"

def rms_norm(x, g):
    xf = x.astype(jnp.float32)
    y = xf * lax.rsqrt(jnp.mean(xf * xf, axis=-1, keepdims=True) + RMS_EPS)
    return (y * g.astype(jnp.float32)).astype(x.dtype)

def rope(t, pos):
    half = HEAD_DIM // 2
    inv = ROPE_THETA ** (-jnp.arange(half, dtype=jnp.float32) / half)
    ang = pos.astype(jnp.float32)[:, None] * inv[None, :]
    cos = jnp.cos(ang)[None, :, None, :]
    sin = jnp.sin(ang)[None, :, None, :]
    tf = t.astype(jnp.float32)
    t1, t2 = tf[..., :half], tf[..., half:]
    out = jnp.concatenate([t1 * cos - t2 * sin, t2 * cos + t1 * sin], axis=-1)
    return out.astype(t.dtype)

def band_chunks(t):
    b, s = t.shape[:2]
    n = s // CHUNK
    tc = t.reshape((b, n, CHUNK) + t.shape[2:])
    pad = [(0, 0), (WINDOW_CHUNKS - 1, 0)] + [(0, 0)] * (tc.ndim - 2)
    tp = jnp.pad(tc, pad)
    return jnp.concatenate([tp[:, j:j + n] for j in range(WINDOW_CHUNKS)], axis=2)

def pool_mixer(h, w, b, scale):
    bsz, s, _ = h.shape
    hg = h.reshape(bsz, s, N_POOL_GROUPS, POOL_GROUP_DIM)
    cs = jnp.cumsum(hg.astype(jnp.float32), axis=1)
    t = jnp.arange(s)
    pooled = []
    for g, win in enumerate(POOL_WINDOWS):
        c = cs[:, :, g]
        lagged = jnp.pad(c, ((0, 0), (win, 0), (0, 0)))[:, :s]
        cnt = jnp.minimum(t + 1, win).astype(jnp.float32)[None, :, None]
        pooled.append((c - lagged) / cnt)
    pooled = jnp.stack(pooled, axis=2).astype(h.dtype) - hg
    mixed = jnp.einsum('bsgc,gcd->bsgd', pooled, w) + b
    return mixed.reshape(bsz, s, D_MODEL) * scale

def shared_kv(h, w_kv, b_kv, pos):
    bsz, s, _ = h.shape
    kv = h @ w_kv + b_kv
    k, v = jnp.split(kv, 2, axis=-1)
    k = rope(k.reshape(bsz, s, N_KV_HEADS, HEAD_DIM), pos)
    v = v.reshape(bsz, s, N_KV_HEADS, HEAD_DIM)
    return band_chunks(k), band_chunks(v)

def swa_sink_attention(h, k_band, v_band, mask, w_q, b_q, sinks, w_o, b_o, pos):
    bsz, s, _ = h.shape
    n = s // CHUNK
    q = rope((h @ w_q + b_q).reshape(bsz, s, N_Q_HEADS, HEAD_DIM), pos)
    q = q.reshape(bsz, n, CHUNK, N_KV_HEADS, Q_PER_KV, HEAD_DIM)
    sc = jnp.einsum('bnqkgd,bnskd->bnkgqs', q, k_band,
                    preferred_element_type=jnp.float32) * (HEAD_DIM ** -0.5)
    sc = jnp.where(mask[None, :, None, None, None, :], sc, -jnp.inf)
    sink = sinks.astype(jnp.float32).reshape(N_KV_HEADS, Q_PER_KV)[None, None, :, :, None, None]
    m = jnp.maximum(jnp.max(sc, axis=-1, keepdims=True), sink)
    p = jnp.exp(sc - m)
    denom = jnp.sum(p, axis=-1, keepdims=True) + jnp.exp(sink - m)
    p = (p / denom).astype(v_band.dtype)
    o = jnp.einsum('bnkgqs,bnskd->bnqkgd', p, v_band).reshape(bsz, s, N_Q_HEADS * HEAD_DIM)
    return o @ w_o + b_o

def swiglu(h, w1, w3, w2):
    return (jax.nn.silu(h @ w1) * (h @ w3)) @ w2

def moe_swiglu(h, w_router, w1, w3, w2):
    bsz, s, d = h.shape
    xt = h.reshape(-1, d)
    logits = (xt @ w_router).astype(jnp.float32)
    top_val, top_idx = lax.top_k(logits, TOP_K)
    gate = jax.nn.softmax(top_val, axis=-1)
    combine = jnp.sum(jax.nn.one_hot(top_idx, N_EXPERTS, dtype=jnp.float32)
                      * gate[..., None], axis=1)
    y = jnp.zeros(xt.shape, jnp.float32)
    for e in range(N_EXPERTS):
        y = y + combine[:, e:e + 1] * swiglu(xt, w1[e], w3[e], w2[e]).astype(jnp.float32)
    return y.astype(h.dtype).reshape(bsz, s, d)

def setup_inputs(seed: int = 0) -> dict:
    key = jax.random.key(seed)
    ks = jax.random.split(key, 24)

    def nrm(k, shape, scale):
        return jax.random.normal(k, shape, jnp.float32) * scale

    def gain(k, shape):
        return 1.0 + 0.02 * jax.random.normal(k, shape, jnp.float32)

    qd = N_Q_HEADS * HEAD_DIM
    kvd = 2 * N_KV_HEADS * HEAD_DIM
    return {
        "x": nrm(ks[0], (BATCH, SEQ, D_MODEL), 1.0),
        "norm_mix": gain(ks[1], (DEPTH, D_MODEL)),
        "norm_ffn": gain(ks[2], (DEPTH, D_MODEL)),
        "pool_w": nrm(ks[3], (N_A_LAYERS, N_POOL_GROUPS, POOL_GROUP_DIM, POOL_GROUP_DIM), POOL_GROUP_DIM ** -0.5),
        "pool_b": nrm(ks[4], (N_A_LAYERS, N_POOL_GROUPS, POOL_GROUP_DIM), 0.02),
        "pool_scale": gain(ks[5], (N_A_LAYERS, D_MODEL)),
        "norm_kv": gain(ks[6], (D_MODEL,)),
        "w_kv": nrm(ks[7], (D_MODEL, kvd), D_MODEL ** -0.5),
        "b_kv": nrm(ks[8], (kvd,), 0.02),
        "w_q": nrm(ks[9], (N_B_LAYERS, D_MODEL, qd), D_MODEL ** -0.5),
        "b_q": nrm(ks[10], (N_B_LAYERS, qd), 0.02),
        "attn_sinks": nrm(ks[11], (N_B_LAYERS, N_Q_HEADS), 0.5),
        "w_o": nrm(ks[12], (N_B_LAYERS, qd, D_MODEL), qd ** -0.5),
        "b_o": nrm(ks[13], (N_B_LAYERS, D_MODEL), 0.02),
        "ffn_w1": nrm(ks[14], (N_DENSE_LAYERS, D_MODEL, D_FF), D_MODEL ** -0.5),
        "ffn_w3": nrm(ks[15], (N_DENSE_LAYERS, D_MODEL, D_FF), D_MODEL ** -0.5),
        "ffn_w2": nrm(ks[16], (N_DENSE_LAYERS, D_FF, D_MODEL), D_FF ** -0.5),
        "router_w": nrm(ks[17], (N_MOE_LAYERS, D_MODEL, N_EXPERTS), D_MODEL ** -0.5),
        "moe_w1": nrm(ks[18], (N_MOE_LAYERS, N_EXPERTS, D_MODEL, D_FF), D_MODEL ** -0.5),
        "moe_w3": nrm(ks[19], (N_MOE_LAYERS, N_EXPERTS, D_MODEL, D_FF), D_MODEL ** -0.5),
        "moe_w2": nrm(ks[20], (N_MOE_LAYERS, N_EXPERTS, D_FF, D_MODEL), D_FF ** -0.5),
        "norm_final": gain(ks[21], (D_MODEL,)),
    }

def reference(x, norm_mix, norm_ffn, pool_w, pool_b, pool_scale, norm_kv, w_kv, b_kv,
              w_q, b_q, attn_sinks, w_o, b_o, ffn_w1, ffn_w3, ffn_w2,
              router_w, moe_w1, moe_w3, moe_w2, norm_final):
    s = x.shape[1]
    n = s // CHUNK
    pos = jnp.arange(s, dtype=jnp.int32)
    key_chunk = jnp.arange(WINDOW_CHUNKS * CHUNK) // CHUNK
    mask = (jnp.arange(n)[:, None] - (WINDOW_CHUNKS - 1) + key_chunk[None, :]) >= 0
    k_band = v_band = None
    for i in range(DEPTH):
        h = rms_norm(x, norm_mix[i])
        if i < N_A_LAYERS:
            x = x + pool_mixer(h, pool_w[i], pool_b[i], pool_scale[i])
        else:
            j = i - N_A_LAYERS
            x = x + swa_sink_attention(h, k_band, v_band, mask, w_q[j], b_q[j],
                                       attn_sinks[j], w_o[j], b_o[j], pos)
        h = rms_norm(x, norm_ffn[i])
        if i % 2 == 0:
            d = i // 2
            x = x + swiglu(h, ffn_w1[d], ffn_w3[d], ffn_w2[d])
        else:
            m = i // 2
            x = x + moe_swiglu(h, router_w[m], moe_w1[m], moe_w3[m], moe_w2[m])
        if i == N_A_LAYERS - 1:
            k_band, v_band = shared_kv(rms_norm(x, norm_kv), w_kv, b_kv, pos)
    return rms_norm(x, norm_final)


_drawn_inputs = setup_inputs


def setup_inputs(seed=0):
    import zlib

    import numpy as np

    out = dict(_drawn_inputs(seed))
    spreads = {}
    factors = {'norm_kv': 3.549,
     'b_q': 2.689,
     'attn_sinks': 18.581,
     'norm_final': 20.77,
     'b_kv': 3.382,
     'b_o': 5.066}
    for name, (base, spread) in spreads.items():
        noise = np.random.default_rng([zlib.crc32(name.encode()), seed]).standard_normal(out[name].shape)
        drawn = base * np.exp(spread * noise) if base else spread * noise
        out[name] = __import__('jax').numpy.asarray(drawn.astype(out[name].dtype))
    for name, factor in factors.items():
        out[name] = (out[name] * factor).astype(out[name].dtype)
    return out
```

```python
import numpy as np
from contextlib import ExitStack

import concourse.bass as bass
from concourse import mybir

F32 = mybir.dt.float32
F32R = mybir.dt.float32r
I32 = mybir.dt.int32
ALU = mybir.AluOpType
ACT = mybir.ActivationFunctionType
AX_X = mybir.AxisListType.X

P = 128
SEQ = 256
D = 1024
F = 3584
E = 8
HD = 64
NH = 16
CHUNK = 64
WINDOWS = (2, 4, 8, 16)
NT = SEQ // P
DT = D // P
CW = 512
NC = F // CW
UNIT = 2048
RING = 14
NHI = 3
EPS = 1e-5
MASKED = -1e30

FFN_UNITS = []
for _c in range(NC + 1):
    if _c < NC:
        FFN_UNITS += [("w1", _c, 0), ("w1", _c, 1), ("w3", _c, 0), ("w3", _c, 1)]
    if _c > 0:
        FFN_UNITS += [("w2", _c - 1, 0), ("w2", _c - 1, 1)]
NU = len(FFN_UNITS)
AT = {key: j for j, key in enumerate(FFN_UNITS)}
TURN = {c: AT[("w2", c - 1, 0)] if c else AT[("w3", 0, 1)] for c in range(NC)}
GATHER_AT = AT[("w2", NC - 2, 1)]
PICK_AT = AT[("w3", 2, 0)]

U_BAND, U_POOLW = 0, 1
U_DENSE = 2
U_KV = U_DENSE + NU
U_Q = U_KV + 1
U_O = U_Q + 4
U_MOE = (U_O + 4, U_O + 4 + E * NU)
assert NU % RING == 0 and NU % NHI == 0

C_ID, C_TRI, C_ONE, C_IOTA = 0, P, 2 * P, 3 * P
C_MASK = (4 * P, 5 * P)
C_COS, C_SIN = 7 * P, 9 * P
C_N = 11 * P


def shape_constants():
    t = np.arange(SEQ)
    table = np.zeros((P, C_N), np.float32)
    table[:, C_ID:C_ID + P] = np.eye(P)
    table[:, C_TRI:C_TRI + P] = np.triu(np.ones((P, P)))
    table[:, C_ONE:C_ONE + P] = 1.0
    table[:, C_IOTA:C_IOTA + P] = np.arange(P)[None, :]
    for q in range(NT):
        chunk_q = (t[q * P:(q + 1) * P] // CHUNK)[:, None]
        chunk_k = (t[:(q + 1) * P] // CHUNK)[None, :]
        seen = (chunk_k <= chunk_q) & (chunk_k >= chunk_q - 1)
        table[:, C_MASK[q]:C_MASK[q] + (q + 1) * P] = np.where(seen, 0.0, MASKED)
    half = HD // 2
    inv = (np.float32(10000.0) ** (-np.arange(half, dtype=np.float32) / half)).astype(np.float32)
    ang = t.astype(np.float32)[None, :] * inv[:, None]
    row = np.arange(P) % half
    table[:, C_COS:C_COS + SEQ] = np.cos(ang)[row]
    sign = np.where(np.arange(P) % HD < half, 1.0, -1.0)[:, None]
    table[:, C_SIN:C_SIN + SEQ] = np.sin(ang)[row] * sign
    bands = np.zeros((len(WINDOWS), SEQ, SEQ), np.float32)
    for g, win in enumerate(WINDOWS):
        back = t[None, :] - t[:, None]
        mean = ((back >= 0) & (back < win)) / np.minimum(t + 1, win)[None, :].astype(np.float32)
        bands[g] = mean.astype(np.float32) - np.eye(SEQ, dtype=np.float32)
    bands = bands.reshape(len(WINDOWS), NT, P, SEQ).transpose(2, 0, 1, 3)
    return table, np.ascontiguousarray(bands.reshape(P, -1))


def trunk_program(nc, x, norm_mix, norm_ffn, pool_w, pool_b, pool_scale, norm_kv, w_kv, b_kv, w_q, b_q,
                  attn_sinks, w_o, b_o, ffn_w1, ffn_w3, ffn_w2, router_w, moe_w1, moe_w3, moe_w2,
                  norm_final, table, bands, out):
    ctx = ExitStack()
    with ctx:
        K = 1024
        arena_bytes = (RING + NHI) * UNIT * 4 + 64 * K + C_N * 4 + 2 * K
        arena = ctx.enter_context(nc.sbuf_tensor("arena", [P, arena_bytes // 4], F32))
        base = nc.sbuf_base - arena_bytes
        end = [base]

        def at(name, shape, dtype, offset):
            return nc.alloc_sbuf_tensor_at(name, shape, dtype, offset=offset)

        def place(nbytes):
            end[0] += nbytes
            assert end[0] <= base + arena_bytes
            return end[0] - nbytes

        o_raw = place(RING * UNIT * 4)
        raw = [at(f"raw{r}", [P, UNIT], F32, o_raw + r * UNIT * 4) for r in range(RING)]
        low = [at(f"low{r}", [P, UNIT], F32R, o_raw + r * UNIT * 4) for r in range(RING)]
        high = [at(f"high{r}", [P, UNIT], F32R, place(UNIT * 4)) for r in range(NHI)]
        x_res = at("x_res", [P, NT, D], F32, place(8 * K))
        o_a = place(16 * K)
        o_b = place(16 * K)
        o_w = place(20 * K)
        row_bc = at("row_bc", [P, D], F32, place(4 * K))
        consts = at("consts", [P, C_N], F32, place(C_N * 4))
        o_s = place(2 * K)

        a_hi = at("a_hi", [P, DT, SEQ], F32R, o_a)
        a_lo = at("a_lo", [P, DT, SEQ], F32R, o_a + 8 * K)
        xg_hi = at("xg_hi", [P, DT, P], F32R, o_a)
        xg_lo = at("xg_lo", [P, DT, P], F32R, o_a + 8 * K)
        probs = at("probs", [P, 2, CW], F32, o_a)
        probs_t = at("probs_t", [P, 2, CW], F32, o_a + 8 * K)
        b_hi = at("b_hi", [P, 2, NT, CW], F32R, o_b)
        b_lo = at("b_lo", [P, 2, NT, CW], F32R, o_b + 8 * K)
        pool_rows = at("pool_rows", [P, 2, D], F32, o_b)
        pool_bs = at("pool_bs", [P, D], F32, o_b + 8 * K)
        pool_y = at("pool_y", [P, D], F32, o_b + 12 * K)
        kv_hi = b_hi[:].rearrange("p a b c -> p (a b c)").rearrange("p (d t) -> p d t", d=DT)
        kv_lo = b_lo[:].rearrange("p a b c -> p (a b c)").rearrange("p (d t) -> p d t", d=DT)
        ot_hi, ot_lo = kv_hi, kv_lo
        xs_hi = b_hi[:].rearrange("p a b c -> p (a b c)").rearrange("p (t d) -> p t d", t=NT)
        xs_lo = b_lo[:].rearrange("p a b c -> p (a b c)").rearrange("p (t d) -> p t d", t=NT)
        pooled_t = at("pooled_t", [P, DT, SEQ], F32, o_w)
        xn_t = at("xn_t", [P, DT, SEQ], F32, o_w)
        q_t = at("q_t", [P, DT, SEQ], F32, o_w)
        h_t = at("h_t", [P, DT, SEQ], F32, o_w)
        xn = at("xn", [P, NT, D], F32, o_w + 8 * K)
        rope_x = at("rope_x", [P, 2, 2, SEQ], F32, o_w + 8 * K)
        rope_y = at("rope_y", [P, 2, SEQ], F32, o_w + 12 * K)
        rope_z = at("rope_z", [P, 2, SEQ], F32, o_w + 14 * K)
        hidden = at("hidden", [P, NT, CW], F32, o_w + 16 * K)
        k_t = at("k_t", [P, 2, SEQ], F32, o_w + 16 * K)
        v_tok = at("v_tok", [P, NT, P], F32, o_w + 18 * K)
        hm_hi = at("hm_hi", [P, 2, CW], F32R, o_w)
        hm_lo = at("hm_lo", [P, 2, CW], F32R, o_w + 4 * K)
        y_hi = at("y_hi", [P, D], F32R, o_w + 8 * K)
        y_lo = at("y_lo", [P, D], F32R, o_w + 12 * K)
        pick = at("pick", [P, NT, P], F32R, o_w + 18 * K)
        pick_t = at("pick_t", [P, SEQ], F32R, o_w + 19 * K)
        smalls = at("smalls", [P, 512], F32, o_s)
        small_at = [0]

        def small(n):
            small_at[0] += n
            assert small_at[0] <= 512
            return smalls[:, small_at[0] - n:small_at[0]]

        NV = 5 * DT + 1
        gains = small(NV)
        sinks = small(NH)
        neg_sinks = small(NH)
        sumsq = small(NT)
        var = small(NT)
        std = small(NT)
        rstd = small(NT)
        maxima = small(2 * 4)
        neg_max = small(2 * 4)
        sums = small(2 * 4)
        sink_in = small(2 * 4)
        sink_exp = small(2 * 4)
        denom = small(4)
        recip = small(2 * 4)
        r_w = small(DT * E)
        logits = small(NT * E)
        top = small(NT * 8)
        eq = small(NT * E)
        run = small(NT * E)
        first = small(NT * E)
        second = small(NT * E)
        rest = small(NT * E)
        chosen = small(NT * E)
        gate_w = small(NT * 4)
        position = small(2 * NT * (E + 1))
        combine = small(NT * (E + 1))
        zeros8 = small(E)
        over = small(2)
        over_flag = small(1).bitcast(I32)
        vec_rows = at("vec_rows", [NV, P], F32, o_a)
        b_v = at("b_v", [P, P], F32, o_w + 19 * K)

        banks = [ctx.enter_context(nc.psum_tensor(f"bank{i}", [P, CW], F32)) for i in range(8)]
        UP1, UP3 = (0, 1), (2, 3)
        OUT = ((4, 5), (6, 7))
        TURN_BANK, PICK_BANK, GATHER = 1, 3, (6, 7)
        PROJ = ((0, 1), (2, 3))

        def view3(t, n):
            return t[:].rearrange("p (a b) -> p a b", a=n)

        ident = consts[:, C_ID:C_ID + P]
        pos4 = position[:].rearrange("p (s t e) -> p s t e", s=2, t=NT)
        comb3 = view3(combine, NT)

        def sem(name):
            return ctx.enter_context(nc.semaphore(name))

        landed = [sem(f"landed{r}") for r in range(RING)]
        split_hi, split_lo = sem("split_hi"), sem("split_lo")
        unit_used = sem("unit_used")
        x_in, consts_in, vec_in, pool_in = sem("x_in"), sem("consts_in"), sem("vec_in"), sem("pool_in")
        misc_in, bo_in, bv_in = sem("misc_in"), sem("bo_in"), sem("bv_in")
        gn_in, gf_in, out_done = sem("gn_in"), sem("gf_in"), sem("out_done")
        sumsq_ready, var_ready, std_ready = sem("sumsq_ready"), sem("var_ready"), sem("std_ready")
        xn_ready = sem("xn_ready")
        x_ready = sem("x_ready")
        stream_done = sem("stream_done")
        vec_turned, gains_ready = sem("vec_turned"), sem("gains_ready")
        pool_ready, pooled, pooled_out, mixed = sem("pool_ready"), sem("pooled"), sem("pooled_out"), sem("mixed")
        turned, a_hi_ready, a_lo_ready = sem("turned"), sem("a_hi_ready"), sem("a_lo_ready")
        activated, gated, hidden_turned = sem("activated"), sem("gated"), sem("hidden_turned")
        hidden_hi, hidden_lo = sem("hidden_hi"), sem("hidden_lo")
        xn_t_ready = sem("xn_t_ready")
        kv_hi_ready, kv_lo_ready, kv_done, v_out = sem("kv_hi_ready"), sem("kv_lo_ready"), sem("kv_done"), sem("v_out")
        biased, cosined, roped = sem("biased"), sem("cosined"), sem("roped")
        scored, score_out, max_ready, exped = sem("scored"), sem("score_out"), sem("max_ready"), sem("exped")
        weighted, probs_turned, probs_out, attended = sem("weighted"), sem("probs_turned"), sem("probs_out"), sem("attended")
        ot_hi_ready, ot_lo_ready, bo_added = sem("ot_hi_ready"), sem("ot_lo_ready"), sem("bo_added")
        gained, xs_hi_ready, xs_lo_ready = sem("gained"), sem("xs_hi_ready"), sem("xs_lo_ready")
        h_out, routed, gate_in, gate_exp = sem("h_out"), sem("routed"), sem("gate_in"), sem("gate_exp")
        chosen_ready, counted, flag_ready = sem("chosen_ready"), sem("counted"), sem("flag_ready")
        picked, gathered = sem("picked"), sem("gathered")
        xg_hi_ready, xg_lo_ready = sem("xg_hi_ready"), sem("xg_lo_ready")
        pick_turned, pick_t_ready = sem("pick_turned"), sem("pick_t_ready")
        y_hi_ready, y_lo_ready = sem("y_hi_ready"), sem("y_lo_ready")
        scattered, added = sem("scattered"), sem("added")
        dve_step, pool_step = sem("dve_step"), sem("pool_step")

        x_d = x.rearrange("o (t p) d -> p (o t) d", p=P)
        out_d = out.rearrange("o (t p) d -> p (o t) d", p=P)

        def up_view(w):
            return w.rearrange("o (k p) f -> o p k f", p=P)

        dense = {"w1": up_view(ffn_w1), "w3": up_view(ffn_w3), "w2": up_view(ffn_w2)}
        experts = {n: w.rearrange("o e (k p) f -> (o e) p k f", p=P)
                   for n, w in (("w1", moe_w1), ("w3", moe_w3), ("w2", moe_w2))}

        def bc(row):
            return row.rearrange("(o n) -> o n", o=1).to_broadcast([P, row.shape[0]])

        def ffn_source(views, e, kind, c, half):
            if kind == "w2":
                part = views[kind][bass.ds(e, 1), :, 4 * c + 2 * half:4 * c + 2 * half + 2, :]
            else:
                part = views[kind][bass.ds(e, 1), :, 4 * half:4 * half + 4, c * CW:(c + 1) * CW]
            return part.rearrange("o p k f -> p (o k) f")

        def slot(u):
            return u % RING

        def hslot(u):
            return (u - U_DENSE) % NHI

        def turned_x(d):
            return banks[d // 2][:, (d % 2) * SEQ:(d % 2 + 1) * SEQ]

        def raw3(u, k):
            return raw[slot(u)][:].rearrange("p (k f) -> p k f", k=k)

        def hi3(u, k):
            return high[hslot(u)][:].rearrange("p (k f) -> p k f", k=k)

        def lo3(u, k):
            return low[slot(u)][:].rearrange("p (k f) -> p k f", k=k)

        class Pass:

            def __init__(self, n):
                self.moe = n > 0
                self.tiles = 1 if n else NT
                self.block = n - 1
                self.u0 = U_MOE[n - 1] if n else U_DENSE
                self.k0 = NC + (n - 1) * E * NC if n else 0
                self.x0 = (n - 1) * (E + 1)
                self.p0 = (n - 1) * E

            def units(self, j, e):
                return e * NU + (self.u0 + j) if self.moe else self.u0 + j

            def chunks(self, c, e):
                return e * NC + (self.k0 + c) if self.moe else self.k0 + c

        PASSES = [Pass(0), Pass(1), Pass(2)]

        STEPS = [(0, h, 4) for h in (0, 1, 8, 9)] + [(1, 4 * a + p, 2) for a in range(4) for p in range(2)]
        NS = len(STEPS)

        def heads(i):
            t, h0, n = STEPS[i]
            return [h0 + 2 * k for k in range(n)]

        ROPE = [(1, 4, 5 * DT)] + [(2, 6 + m % 2, 4 * DT + 2 * m) for m in range(4)]

        block = ctx.enter_context(nc.Block())

        @block.sync
        def _(sp):
            def load(u, src, k, used=None):
                used = u - RING + 1 if used is None else used
                if not isinstance(used, int) or used > 0:
                    sp.wait_ge(unit_used, used)
                sp.dma_start(raw3(u, k), src).then_inc(landed[slot(u)], 16)

            sp.dma_start(x_res[:], x_d).then_inc(x_in, 16)
            load(U_BAND, bands.rearrange("p (k f) -> p k f", k=8), 8)
            load(U_POOLW, pool_w.rearrange("o g (k p) f -> p (o g k) f", p=P), 8)
            for j, key in enumerate(FFN_UNITS):
                load(U_DENSE + j, ffn_source(dense, 0, *key), 2 if key[0] == "w2" else 4)
            load(U_KV, w_kv.rearrange("(k p) f -> p k f", p=P), DT)
            for m in range(4):
                load(U_Q + m, w_q[0].rearrange("(k p) f -> p k f", p=P)[:, :, m * SEQ:(m + 1) * SEQ], DT)
            for m in range(4):
                load(U_O + m, w_o[0].rearrange("(k p) f -> p k f", p=P)[:, 2 * m:2 * m + 2, :], 2)

            def expert_loads(ps):
                with sp.Fori(0, E) as e:
                    for j, key in enumerate(FFN_UNITS):
                        load(ps.u0 + j, ffn_source(experts, e, *key), 2 if key[0] == "w2" else 4,
                             ps.units(j - RING + 1, e))

            expert_loads(PASSES[1])
            sp.wait_ge(flag_ready, 1)
            again = sp.value_load(over_flag[0:1, 0:1], min_val=0, max_val=1)
            with sp.If(again > 0):
                expert_loads(PASSES[2])
            for t in range(NT):
                sp.wait_ge(xn_ready, 3 * NT + t + 1)
                sp.dma_start(out_d[:, t, :], xn[:, t, :]).then_inc(out_done, 16)
            sp.wait_ge(out_done, 16 * NT)

        @block.gpsimd
        def _(pool):
            pool.wait_ge(pool_in, 32)
            pool.tensor_tensor(pool_bs[:], pool_rows[:, 0, :], pool_rows[:, 1, :], ALU.mult).then_inc(pool_step, 1)
            pool.wait_ge(pool_step, 1)
            pool.wait_ge(xn_ready, NT)
            for t in range(NT):
                pool.tensor_tensor(x_res[:, t, :], x_res[:, t, :], pool_bs[:], ALU.add).then_inc(pool_ready, 1)
            pool.wait_ge(xn_ready, 3 * NT)
            pool.dma_start(b_v[:], bc(b_kv[P:2 * P])).then_inc(bv_in, 16)
            pool.wait_ge(bo_in, 16)
            for t in range(NT):
                pool.tensor_tensor(x_res[:, t, :], x_res[:, t, :], row_bc[:], ALU.add).then_inc(bo_added, 1)
            for i, (n, _, _) in enumerate(ROPE):
                pool.wait_ge(biased, i + 1)
                if i:
                    pool.wait_ge(roped, i)
                pool.tensor_tensor(rope_y[:, 0:n, :], rope_x[:, i % 2, 0:n, :],
                                   consts[:, C_COS:C_COS + SEQ].unsqueeze(1).to_broadcast([P, n, SEQ]),
                                   ALU.mult).then_inc(cosined, 1)
            pool.wait_ge(bo_added, NT)
            pool.dma_start(row_bc[:], bc(norm_ffn[1])).then_inc(gn_in, 16)
            pool.wait_ge(gained, NT)
            pool.dma_start(row_bc[:], bc(norm_final)).then_inc(gf_in, 16)
            pool.memset(pick_t[:].bitcast(F32), 0.0).then_inc(pick_t_ready, 1)

        @block.tensor
        def _(pe):
            def three_passes(o, s_hi, s_lo, m_hi, m_lo, start, stop):
                pe.matmul(o, s_hi, m_hi, start=start, stop=False)
                pe.matmul(o, s_lo, m_hi, start=False, stop=False)
                return pe.matmul(o, s_hi, m_lo, start=False, stop=stop)

            def turn_stream():
                for d in range(DT):
                    for t in range(NT):
                        at_ = (d % 2) * SEQ + t * P
                        mm = pe.transpose(banks[d // 2][:, at_:at_ + P], xn[:, t, d * P:(d + 1) * P], ident)
                    if d % 2:
                        mm.then_inc(turned, 1)

            def gather():
                for d in range(DT):
                    o = banks[GATHER[d // 4]][:, (d % 4) * P:(d % 4 + 1) * P]
                    for t in range(NT):
                        pe.matmul(o, xs_hi[:, t, d * P:(d + 1) * P], pick[:, t, :], start=t == 0, stop=False)
                        mm = pe.matmul(o, xs_lo[:, t, d * P:(d + 1) * P], pick[:, t, :],
                                       start=False, stop=t == NT - 1)
                mm.then_inc(gathered, 1)

            def scatter():
                for t, pair in enumerate((OUT[0], GATHER)):
                    s = pick_t[:, t * P:(t + 1) * P]
                    for half in range(2):
                        m = slice(half * CW, (half + 1) * CW)
                        pe.matmul(banks[pair[half]][:], s, y_hi[:, m], start=True, stop=False)
                        mm = pe.matmul(banks[pair[half]][:], s, y_lo[:, m], start=False, stop=True)
                    mm.then_inc(scattered, 1)

            def feed_forward(ps, e):
                act_hi, act_lo = (xg_hi, xg_lo) if ps.moe else (a_hi, a_lo)
                for j, (kind, c, half) in enumerate(FFN_UNITS):
                    u = ps.u0 + j
                    pe.wait_ge(split_lo, ps.units(j - U_DENSE + 1, e))
                    if kind == "w1" and half == 0:
                        if ps.moe or c:
                            pe.wait_ge(hidden_lo, ps.chunks(c, e))
                        if c == 0 and ps.moe:
                            pe.wait_ge(xg_lo_ready, e + (ps.x0 + 1))
                        elif c == 0:
                            pe.wait_ge(a_lo_ready, DT)
                    if kind == "w2" and half == 0:
                        pe.wait_ge(hidden_lo, ps.chunks(c + 1, e))
                        if c == 0 and ps.moe:
                            pe.wait_ge(added, e * 2 + (2 * ps.x0 + 1))
                    if kind == "w2":
                        for ft in range(2):
                            i = 2 * half + ft
                            s = slice(i * P, (i + 1) * P)
                            for t in range(ps.tiles):
                                s_hi = hm_hi[:, c % 2, s] if ps.moe else b_hi[:, c % 2, t, s]
                                s_lo = hm_lo[:, c % 2, s] if ps.moe else b_lo[:, c % 2, t, s]
                                for nh in range(2):
                                    m = slice(nh * CW, (nh + 1) * CW)
                                    mm = three_passes(banks[OUT[t][nh]][:], s_hi, s_lo,
                                                      hi3(u, 2)[:, ft, m], lo3(u, 2)[:, ft, m],
                                                      c == 0 and i == 0, c == NC - 1 and i == 3)
                    else:
                        up = UP1 if kind == "w1" else UP3
                        for k in range(4):
                            d = 4 * half + k
                            for t in range(ps.tiles):
                                s = slice(t * P, (t + 1) * P)
                                mm = three_passes(banks[up[t]][:], act_hi[:, d, s], act_lo[:, d, s],
                                                  hi3(u, 4)[:, k, :], lo3(u, 4)[:, k, :], d == 0, d == DT - 1)
                    mm.then_inc(unit_used, 1)
                    if ps.moe and j == TURN[0]:
                        pe.wait_ge(y_lo_ready, e + (ps.x0 + 1))
                        pe.wait_ge(pick_t_ready, e + (ps.p0 + 1))
                        scatter()
                        for t in range(NT):
                            mm = pe.transpose(banks[PICK_BANK][:, t * P:(t + 1) * P],
                                              pick[:, t, :].bitcast(F32), ident)
                        mm.then_inc(pick_turned, 1)
                    for cc in range(NC):
                        if TURN[cc] == j:
                            pe.wait_ge(gated, ps.chunks(cc + 1, e))
                            for t in range(ps.tiles):
                                for i in range(4):
                                    mm = pe.transpose(banks[TURN_BANK if ps.moe else UP1[t]][:, i * P:(i + 1) * P],
                                                      hidden[:, t, i * P:(i + 1) * P], ident)
                            mm.then_inc(hidden_turned, 1)
                    if ps.moe and j == GATHER_AT:
                        pe.wait_ge(picked, e + (ps.x0 + 2))
                        pe.wait_ge(added, e * 2 + (2 * ps.x0 + 2))
                        gather()

            pe.wait_ge(consts_in, 16)
            pe.wait_ge(vec_in, 16 * 6)
            pe.transpose(banks[7][:, 0:NV], vec_rows[:, :], ident[0:NV, 0:NV]).then_inc(vec_turned, 1)

            pe.wait_ge(xn_ready, NT)
            pe.wait_ge(landed[U_BAND], 16)
            band = raw3(U_BAND, 8)
            for d in range(DT):
                for t in range(NT):
                    mm = pe.matmul(banks[d // 2][:, (d % 2) * SEQ:(d % 2 + 1) * SEQ], xn[:, t, d * P:(d + 1) * P],
                                   band[:, (d // 2) * NT + t, :], start=t == 0, stop=t == NT - 1)
                if d % 2:
                    mm.then_inc(pooled, 1)
            pe.wait_ge(pooled, DT // 2)
            pe.wait_ge(landed[U_POOLW], 16)
            pe.wait_ge(gains_ready, 1)
            w = raw3(U_POOLW, 8)
            for g in range(len(WINDOWS)):
                pe.wait_ge(pooled_out, g + 1)
                for t in range(NT):
                    for k in range(2):
                        mm = pe.matmul(banks[OUT[t][g // 2]][:, (g % 2) * SEQ:(g % 2 + 1) * SEQ],
                                       pooled_t[:, 2 * g + k, t * P:(t + 1) * P], w[:, 2 * g + k, :],
                                       start=k == 0, stop=k == 1)
                if g % 2:
                    mm.then_inc(mixed, 1)
            pe.wait_ge(mixed, 2)
            pe.nop().then_inc(unit_used, 2)

            pe.wait_ge(xn_ready, 2 * NT)
            turn_stream()
            feed_forward(PASSES[0], 0)

            pe.wait_ge(xn_ready, 3 * NT)
            turn_stream()
            pe.wait_ge(kv_lo_ready, DT)
            pe.wait_ge(split_lo, U_KV - U_DENSE + 1)
            wh, wl = hi3(U_KV, DT), lo3(U_KV, DT)
            for d in range(DT):
                mm = three_passes(banks[4][:, 0:SEQ], wh[:, d, 0:P], wl[:, d, 0:P], kv_hi[:, d, :], kv_lo[:, d, :],
                                  d == 0, d == DT - 1)
            mm.then_inc(kv_done, 1)
            for t in range(NT):
                s = slice(t * P, (t + 1) * P)
                for d in range(DT):
                    mm = three_passes(banks[5][:, s], kv_hi[:, d, s], kv_lo[:, d, s], wh[:, d, P:2 * P],
                                      wl[:, d, P:2 * P], d == 0, d == DT - 1)
            mm.then_inc(unit_used, 1)
            pe.wait_ge(a_lo_ready, 2 * DT)
            for m in range(4):
                u = U_Q + m
                pe.wait_ge(split_lo, u - U_DENSE + 1)
                if m >= 2:
                    pe.wait_ge(biased, m)
                for n in range(2):
                    for d in range(DT):
                        s = slice(n * P, (n + 1) * P)
                        mm = three_passes(banks[6 + m % 2][:, n * SEQ:(n + 1) * SEQ], hi3(u, DT)[:, d, s],
                                          lo3(u, DT)[:, d, s], a_hi[:, d, :], a_lo[:, d, :], d == 0, d == DT - 1)
                mm.then_inc(unit_used, 1)

            def scores(i):
                t, h0, n = STEPS[i]
                nk = (t + 1) * P
                rows = slice(HD * (h0 % 2), HD * (h0 % 2) + HD)
                if i >= 2:
                    pe.wait_ge(score_out, i - 1)
                for a, h in enumerate(heads(i)):
                    mm = pe.matmul(banks[i % 2][:, a * nk:(a + 1) * nk], q_t[rows, h // 2, t * P:(t + 1) * P],
                                   k_t[rows, h // (NH // 2), 0:nk], start=True, stop=True)
                mm.then_inc(scored, 1)

            def turn_probs(i):
                pe.wait_ge(weighted, i + 1)
                if i >= 2:
                    pe.wait_ge(probs_out, i - 1)
                for a in range(4):
                    mm = pe.transpose(banks[2 + i % 2][:, a * P:(a + 1) * P], probs[:, i % 2, a * P:(a + 1) * P], ident)
                mm.then_inc(probs_turned, 1)

            def attend(i):
                t, h0, n = STEPS[i]
                pe.wait_ge(probs_out, i + 1)
                g = h0 // (NH // 2)
                rows = slice(HD * (h0 % 2), HD * (h0 % 2) + HD)
                for a, h in enumerate(heads(i)):
                    at_ = (h // 2 % 2) * SEQ + t * P
                    for kt in range(t + 1):
                        b = a * (t + 1) + kt
                        mm = pe.matmul(banks[4 + h // 4][rows, at_:at_ + P], v_tok[:, kt, g * HD:(g + 1) * HD],
                                       probs_t[:, i % 2, b * P:(b + 1) * P], start=kt == 0, stop=kt == t)
                mm.then_inc(attended, 1)

            pe.wait_ge(roped, len(ROPE))
            pe.wait_ge(v_out, NT)
            for i in range(NS + 2):
                if i < NS:
                    scores(i)
                if 1 <= i <= NS:
                    turn_probs(i - 1)
                if i >= 2:
                    attend(i - 2)

            pe.wait_ge(ot_lo_ready, 4)
            for m in range(4):
                u = U_O + m
                pe.wait_ge(split_lo, u - U_DENSE + 1)
                for k in range(2):
                    d = 2 * m + k
                    for t in range(NT):
                        s = slice(t * P, (t + 1) * P)
                        for nh in range(2):
                            c = slice(nh * CW, (nh + 1) * CW)
                            mm = three_passes(banks[PROJ[t][nh]][:], ot_hi[:, d, s], ot_lo[:, d, s],
                                              hi3(u, 2)[:, k, c], lo3(u, 2)[:, k, c], d == 0, d == DT - 1)
                mm.then_inc(unit_used, 1)

            pe.wait_ge(gained, NT)
            turn_stream()
            pe.wait_ge(h_out, DT // 2)
            pe.wait_ge(misc_in, 32)
            for t in range(NT):
                for d in range(DT):
                    mm = pe.matmul(banks[4][:, t * E:(t + 1) * E], h_t[:, d, t * P:(t + 1) * P],
                                   r_w[:, d * E:(d + 1) * E], start=d == 0, stop=d == DT - 1)
            mm.then_inc(routed, 1)
            pe.wait_ge(chosen_ready, 1)
            tri, ones = consts[:, C_TRI:C_TRI + P], consts[:, C_ONE:C_ONE + P]
            c0, c1 = chosen[:, 0:E], chosen[:, E:2 * E]
            pe.matmul(banks[5][:, 0:E], tri, c0, start=True, stop=True)
            pe.matmul(banks[5][:, E:2 * E], tri, c1, start=True, stop=False)
            pe.matmul(banks[5][:, E:2 * E], ones, c0, start=False, stop=True)
            pe.matmul(banks[5][:, 2 * E:3 * E], ones, c0, start=True, stop=False)
            pe.matmul(banks[5][:, 2 * E:3 * E], ones, c1, start=False, stop=True).then_inc(counted, 1)

            def expert_pass(ps):
                pe.wait_ge(picked, ps.x0 + 1)
                pe.wait_ge(xs_lo_ready, NT)
                if ps.x0:
                    pe.wait_ge(added, 2 * ps.x0)
                gather()
                with pe.Fori(0, E) as e:
                    feed_forward(ps, e)
                pe.wait_ge(y_lo_ready, ps.x0 + E + 1)
                pe.wait_ge(pick_t_ready, ps.p0 + E + 1)
                scatter()

            expert_pass(PASSES[1])
            pe.wait_ge(flag_ready, 1)
            again = pe.value_load(over_flag[0:1, 0:1], min_val=0, max_val=1)
            with pe.If(again > 0):
                expert_pass(PASSES[2])

        @block.scalar
        def _(act):
            def split(u, ps=None, j=0, e=0):
                r = slot(u)
                if ps is not None and ps.moe:
                    act.wait_ge(landed[r], e * (16 * NU // RING) + 16 * (u // RING + 1))
                    act.wait_ge(unit_used, ps.units(j - NHI + 1, e))
                else:
                    act.wait_ge(landed[r], 16 * (u // RING + 1))
                    if u - NHI >= U_DENSE:
                        act.wait_ge(unit_used, u - NHI + 1)
                act.activation(high[hslot(u)][:], raw[r][:], ACT.Copy).then_inc(split_hi, 1)

            def norm(n, ready, count):
                act.wait_ge(ready, count)
                for t in range(NT):
                    act.activation(xn[:, t, :], x_res[:, t, :], ACT.Square,
                                   accum_out=sumsq[:, t:t + 1]).then_inc(sumsq_ready, 1)
                act.wait_ge(var_ready, n + 1)
                act.activation(std[:], var[:], ACT.Sqrt).then_inc(std_ready, 1)

            def gained_high(row, src, dst, signal, ready=None):
                for d in range(DT):
                    if ready is not None and d % 2 == 0:
                        act.wait_ge(ready, d // 2 + 1)
                    act.activation(dst[:, d, :], src(d), ACT.Copy,
                                   scale=gains[:, row * DT + d:row * DT + d + 1]).then_inc(signal, 1)

            def take_gathered(n):
                act.wait_ge(gathered, n)
                for half in range(2):
                    act.activation(xg_hi[:, 4 * half:4 * half + 4, :].rearrange("p d t -> p (d t)"),
                                   banks[GATHER[half]][:], ACT.Copy).then_inc(xg_hi_ready, 1)

            def take_output():
                for half in range(2):
                    act.activation(y_hi[:, half * CW:(half + 1) * CW], banks[OUT[0][half]][:],
                                   ACT.Copy).then_inc(y_hi_ready, 1)

            def feed_forward(ps, e, ahead=0):
                for j, (kind, c, half) in enumerate(FFN_UNITS):
                    if ps.moe and j == 2:
                        act.wait_ge(unit_used, ps.units(0, e))
                        take_output()
                    for cc in range(NC):
                        if AT[("w1", cc, 1)] + NHI == j:
                            act.wait_ge(unit_used, ps.units(AT[("w1", cc, 1)] + 1, e))
                            if ps.moe or cc:
                                act.wait_ge(hidden_turned, ps.chunks(cc, e))
                            for t in range(ps.tiles):
                                mm = act.activation(hidden[:, t, :], banks[UP1[t]][:], ACT.Silu)
                            mm.then_inc(activated, 1)
                    if ps.moe and j == TURN[0] + NHI:
                        act.wait_ge(pick_turned, e + (ps.p0 + 1))
                        act.activation(pick_t[:], banks[PICK_BANK][:, 0:SEQ], ACT.Copy).then_inc(pick_t_ready, 1)
                    for cc in range(NC):
                        if TURN[cc] + NHI == j:
                            act.wait_ge(hidden_turned, ps.chunks(cc + 1, e))
                            for t in range(ps.tiles):
                                dst = hm_hi[:, cc % 2, :] if ps.moe else b_hi[:, cc % 2, t, :]
                                mm = act.activation(dst, banks[TURN_BANK if ps.moe else UP1[t]][:], ACT.Copy)
                            mm.then_inc(hidden_hi, 1)
                    if j >= ahead:
                        split(ps.u0 + j, ps, j, e)
                if ps.moe:
                    take_gathered(e + (ps.x0 + 2))

            act.dma_start(consts[:], table).then_inc(consts_in, 16)
            for i, v in enumerate((norm_mix[0], norm_ffn[0], norm_kv, norm_mix[1], b_q[0])):
                act.dma_start(vec_rows[i * DT:(i + 1) * DT, :], v.rearrange("(d p) -> d p", p=P)).then_inc(vec_in, 16)
            act.dma_start(vec_rows[5 * DT:NV, :], b_kv[0:P].rearrange("(d p) -> d p", p=P)).then_inc(vec_in, 16)
            act.dma_start(pool_rows[:, 0, :], bc(pool_b.rearrange("o g d -> (o g d)"))).then_inc(pool_in, 16)
            act.dma_start(pool_rows[:, 1, :], bc(pool_scale[0])).then_inc(pool_in, 16)
            act.dma_start(row_bc[:], bc(b_o[0])).then_inc(bo_in, 16)
            act.dma_start(sinks[:], bc(attn_sinks[0])).then_inc(misc_in, 16)
            act.dma_start(view3(r_w, DT), router_w[0].rearrange("(k p) e -> p k e", p=P)).then_inc(misc_in, 16)

            norm(0, x_in, 16)
            for i in range(NHI):
                split(U_DENSE + i)
            norm(1, x_ready, NT)
            gained_high(1, turned_x, a_hi, a_hi_ready, turned)
            feed_forward(PASSES[0], 0, ahead=NHI)

            for i in range(NHI):
                split(U_KV + i)
            norm(2, x_ready, 2 * NT)
            for b in range(4):
                act.wait_ge(turned, DT // 2 + b + 1)
                act.activation(xn_t[:, 2 * b:2 * b + 2, :].rearrange("p d t -> p (d t)"), banks[b][:],
                               ACT.Copy).then_inc(xn_t_ready, 1)
            act.wait_ge(xn_t_ready, 4)
            gained_high(2, lambda d: xn_t[:, d, :], kv_hi, kv_hi_ready)
            gained_high(3, lambda d: xn_t[:, d, :], a_hi, a_hi_ready)
            for i, (n, b, col) in enumerate(ROPE):
                if i:
                    act.wait_ge(unit_used, U_KV + 1 + i)
                else:
                    act.wait_ge(kv_done, 1)
                if i >= 2:
                    act.wait_ge(roped, i - 1)
                for k in range(n):
                    mm = act.activation(rope_x[:, i % 2, k, :], banks[b][:, k * SEQ:(k + 1) * SEQ], ACT.Identity,
                                        bias=gains[:, col + k:col + k + 1])
                mm.then_inc(biased, 1)
                if NHI + i < 5 + NHI:
                    split(U_KV + NHI + i)

            def exponentials(i):
                t, h0, n = STEPS[i]
                nk = (t + 1) * P
                s = 4 * (i % 2)
                act.wait_ge(max_ready, i + 1)
                if i >= 2:
                    act.wait_ge(weighted, i - 1)
                for a in range(n):
                    row = probs[:, i % 2, a * nk:(a + 1) * nk]
                    act.activation(row, row, ACT.Exp, bias=neg_max[:, s + a:s + a + 1], scale=HD ** -0.5,
                                   accum_out=sums[:, s + a:s + a + 1])
                act.activation(sink_exp[:, s:s + n], sink_in[:, s:s + n], ACT.Exp).then_inc(exped, 1)

            def take_probs(i):
                act.wait_ge(probs_turned, i + 1)
                if i >= 2:
                    act.wait_ge(attended, i - 1)
                act.activation(probs_t[:, i % 2, :], banks[2 + i % 2][:], ACT.Copy).then_inc(probs_out, 1)

            for i in range(NS + 1):
                if i < NS:
                    exponentials(i)
                if i >= 1:
                    take_probs(i - 1)
            act.wait_ge(attended, NS)
            for b in range(4):
                act.activation(ot_hi[:, 2 * b:2 * b + 2, :].rearrange("p d t -> p (d t)"), banks[4 + b][:],
                               ACT.Copy).then_inc(ot_hi_ready, 1)
            split(U_O + 3)

            norm(3, x_ready, 3 * NT)
            for t in range(NT):
                act.wait_ge(gained, t + 1)
                act.activation(xs_hi[:, t, :], xn[:, t, :], ACT.Copy).then_inc(xs_hi_ready, 1)
            for b in range(4):
                act.wait_ge(turned, (DT // 2) * 2 + b + 1)
                act.activation(h_t[:, 2 * b:2 * b + 2, :].rearrange("p d t -> p (d t)"), banks[b][:],
                               ACT.Copy).then_inc(h_out, 1)
            act.wait_ge(gate_in, 1)
            act.activation(gate_w[:, 2:4], gate_w[:, 0:2], ACT.Exp).then_inc(gate_exp, 1)

            def expert_pass(ps):
                take_gathered(ps.x0 + 1)
                with act.Fori(0, E) as e:
                    feed_forward(ps, e)
                act.wait_ge(unit_used, ps.u0 + E * NU)
                take_output()

            expert_pass(PASSES[1])
            act.wait_ge(flag_ready, 1)
            again = act.value_load(over_flag[0:1, 0:1], min_val=0, max_val=1)
            with act.If(again > 0):
                expert_pass(PASSES[2])

            norm(4, stream_done, 1)

        @block.vector
        def _(dve):
            steps = [0]

            def step(instruction):
                steps[0] += 1
                instruction.then_inc(dve_step, 1)
                dve.wait_ge(dve_step, steps[0])

            def split(u, ps=None, j=0, e=0):
                dve.wait_ge(split_hi, ps.units(j - U_DENSE + 1, e) if ps else u - U_DENSE + 1)
                dve.tensor_tensor(low[slot(u)][:], raw[slot(u)][:], high[hslot(u)][:].bitcast(F32),
                                  ALU.subtract).then_inc(split_lo, 1)

            def norm(n):
                dve.wait_ge(sumsq_ready, NT * (n + 1))
                dve.tensor_scalar(var[:], sumsq[:], 1.0 / D, EPS, ALU.mult, ALU.add).then_inc(var_ready, 1)
                dve.wait_ge(std_ready, n + 1)
                step(dve.reciprocal(rstd[:], std[:]))

            def normalise(n):
                norm(n)
                for t in range(NT):
                    dve.tensor_scalar(xn[:, t, :], x_res[:, t, :], rstd[:, t:t + 1], None,
                                      ALU.mult).then_inc(xn_ready, 1)

            def gained_low(row, src, hi, lo, ready, before, signal):
                for d in range(DT):
                    if d % 2 == 0:
                        dve.wait_ge(ready, before + d + 2)
                    dve.scalar_tensor_tensor(lo[:, d, :], src(d),
                                             gains[:, row * DT + d:row * DT + d + 1], hi[:, d, :].bitcast(F32),
                                             ALU.mult, ALU.subtract).then_inc(signal, 1)

            def take_gathered(n):
                for half in range(2):
                    dve.wait_ge(xg_hi_ready, n + (half + 1))
                    s = slice(4 * half, 4 * half + 4)
                    mm = dve.tensor_tensor(xg_lo[:, s, :].rearrange("p d t -> p (d t)"), banks[GATHER[half]][:],
                                           xg_hi[:, s, :].bitcast(F32).rearrange("p d t -> p (d t)"), ALU.subtract)
                mm.then_inc(xg_lo_ready, 1)

            def take_output(n):
                for half in range(2):
                    dve.wait_ge(y_hi_ready, n + (half + 1))
                    s = slice(half * CW, (half + 1) * CW)
                    mm = dve.tensor_tensor(y_lo[:, s], banks[OUT[0][half]][:], y_hi[:, s].bitcast(F32), ALU.subtract)
                mm.then_inc(y_lo_ready, 1)

            def pick_tokens(ps, expert, before):
                for t in range(NT):
                    mm = dve.tensor_scalar(pick[:, t, :], consts[:, C_IOTA:C_IOTA + P],
                                           pos4[:, ps.block, t, expert], None, ALU.is_equal)
                mm.then_inc(picked, 1)

            def add_scattered(ps, expert, n):
                for t, pair in enumerate((OUT[0], GATHER)):
                    dve.wait_ge(scattered, n + (t + 1))
                    for half in range(2):
                        s = slice(half * CW, (half + 1) * CW)
                        mm = dve.scalar_tensor_tensor(x_res[:, t, s], banks[pair[half]][:], comb3[:, t, expert],
                                                      x_res[:, t, s], ALU.mult, ALU.add)
                    mm.then_inc(added, 1)

            def feed_forward(ps, e, ahead=0):
                for j, (kind, c, half) in enumerate(FFN_UNITS):
                    if ps.moe and j == 2:
                        take_output(e * 2 + 2 * ps.x0)
                    for cc in range(NC):
                        if AT[("w3", cc, 1)] + NHI == j:
                            dve.wait_ge(unit_used, ps.units(AT[("w3", cc, 1)] + 1, e))
                            dve.wait_ge(activated, ps.chunks(cc + 1, e))
                            for t in range(ps.tiles):
                                mm = dve.tensor_tensor(hidden[:, t, :], hidden[:, t, :], banks[UP3[t]][:], ALU.mult)
                            mm.then_inc(gated, 1)
                    if ps.moe and j == TURN[0] + NHI:
                        if ps.x0:
                            dve.wait_ge(added, e * 2 + 2 * ps.x0)
                        add_scattered(ps, bass.ds(e, 1), e * 2 + 2 * ps.x0)
                    for cc in range(NC):
                        if TURN[cc] + NHI == j:
                            dve.wait_ge(hidden_hi, ps.chunks(cc + 1, e))
                            for t in range(ps.tiles):
                                hi = hm_hi[:, cc % 2, :] if ps.moe else b_hi[:, cc % 2, t, :]
                                lo = hm_lo[:, cc % 2, :] if ps.moe else b_lo[:, cc % 2, t, :]
                                mm = dve.tensor_tensor(lo, banks[TURN_BANK if ps.moe else UP1[t]][:],
                                                       hi.bitcast(F32), ALU.subtract)
                            mm.then_inc(hidden_lo, 1)
                    if ps.moe and j == PICK_AT:
                        dve.wait_ge(pick_turned, e + (ps.p0 + 1))
                        pick_tokens(ps, bass.ds(e + 1, 1), e)
                    if j >= ahead:
                        split(ps.u0 + j, ps, j, e)
                if ps.moe:
                    take_gathered(e * 2 + (2 * ps.x0 + 2))

            step(dve.memset(zeros8[:], 0.0))
            step(dve.memset(position[:], -1.0))
            step(dve.memset(combine[:], 0.0))
            dve.wait_ge(x_in, 16)
            normalise(0)
            dve.wait_ge(vec_turned, 1)
            step(dve.tensor_copy(gains[:], banks[7][:, 0:NV]))
            dve.wait_ge(misc_in, 32)
            dve.tensor_scalar(neg_sinks[:], sinks[:], -1.0, None, ALU.mult).then_inc(gains_ready, 1)
            for b in range(4):
                dve.wait_ge(pooled, b + 1)
                for d in (2 * b, 2 * b + 1):
                    mm = dve.tensor_scalar(pooled_t[:, d, :], banks[b][:, (d % 2) * SEQ:(d % 2 + 1) * SEQ],
                                           gains[:, d:d + 1], None, ALU.mult)
                mm.then_inc(pooled_out, 1)
            for i in range(NHI):
                split(U_DENSE + i)
            dve.wait_ge(pool_ready, NT)
            for half in range(2):
                s = slice(half * CW, (half + 1) * CW)
                dve.wait_ge(mixed, half + 1)
                for t in range(NT):
                    y = pool_y[:, t * CW:(t + 1) * CW]
                    step(dve.tensor_tensor(y, banks[OUT[t][half]][:], pool_rows[:, 1, s], ALU.mult))
                    mm = dve.tensor_tensor(x_res[:, t, s], x_res[:, t, s], y, ALU.add)
                    if half:
                        mm.then_inc(x_ready, 1)
                    else:
                        step(mm)

            dve.wait_ge(x_ready, NT)
            normalise(1)
            gained_low(1, turned_x, a_hi, a_lo, a_hi_ready, 0, a_lo_ready)
            feed_forward(PASSES[0], 0, ahead=NHI)
            for i in range(NHI):
                if i == NHI - 1:
                    dve.wait_ge(unit_used, U_KV)
                    for t in range(NT):
                        for half in range(2):
                            s = slice(half * CW, (half + 1) * CW)
                            mm = dve.tensor_tensor(x_res[:, t, s], x_res[:, t, s], banks[OUT[t][half]][:], ALU.add)
                        mm.then_inc(x_ready, 1)
                split(U_KV + i)

            dve.wait_ge(x_ready, 2 * NT)
            normalise(2)
            gained_low(2, lambda d: xn_t[:, d, :], kv_hi, kv_lo, kv_hi_ready, 0, kv_lo_ready)
            gained_low(3, lambda d: xn_t[:, d, :], a_hi, a_lo, a_hi_ready, DT, a_lo_ready)
            sin = consts[:, C_SIN:C_SIN + SEQ]
            half_d = HD // 2
            for i, (n, b, _) in enumerate(ROPE):
                dve.wait_ge(biased, i + 1)
                for r in range(0, P, half_d):
                    to = r ^ half_d
                    mm = dve.tensor_tensor(rope_z[to:to + half_d, 0:n, :], rope_x[r:r + half_d, i % 2, 0:n, :],
                                           sin[r:r + half_d].unsqueeze(1).to_broadcast([half_d, n, SEQ]), ALU.mult)
                step(mm)
                dve.wait_ge(cosined, i + 1)
                if i:
                    m = 2 * (i - 1)
                    dve.tensor_tensor(q_t[:, m:m + 2, :], rope_y[:], rope_z[:], ALU.add).then_inc(roped, 1)
                else:
                    for g in range(2):
                        for to in (0, HD):
                            s = slice(g * HD, (g + 1) * HD)
                            mm = dve.tensor_tensor(k_t[to:to + HD, g, :], rope_y[s, 0, :], rope_z[s, 0, :], ALU.add)
                    mm.then_inc(roped, 1)
                    dve.wait_ge(bv_in, 16)
                    dve.wait_ge(unit_used, U_KV + 1)
                    for t in range(NT):
                        dve.tensor_tensor(v_tok[:, t, :], banks[5][:, t * P:(t + 1) * P], b_v[:],
                                          ALU.add).then_inc(v_out, 1)
                dve.wait_ge(roped, i + 1)
                split(U_KV + NHI + i)

            def head_cols(t_, i):
                h0, n = STEPS[i][1:]
                return t_[:, h0:h0 + 2 * (n - 1) + 1:2]

            def maxima_of(i):
                t, h0, n = STEPS[i]
                nk = (t + 1) * P
                s = slice(4 * (i % 2), 4 * (i % 2) + n)
                sc = probs[:, i % 2, :].rearrange("p (h k) -> p h k", h=n)
                dve.wait_ge(scored, i + 1)
                if i >= 2:
                    dve.wait_ge(probs_turned, i - 1)
                    dve.wait_ge(exped, i - 1)
                mask = consts[:, C_MASK[t]:C_MASK[t] + nk].unsqueeze(1).to_broadcast([P, n, nk])
                dve.tensor_tensor(sc, banks[i % 2][:].rearrange("p (h k) -> p h k", h=n), mask,
                                  ALU.add).then_inc(score_out, 1)
                dve.wait_ge(score_out, i + 1)
                step(dve.tensor_reduce(maxima[:, s], sc, AX_X, ALU.max))
                step(dve.scalar_tensor_tensor(neg_max[:, s], maxima[:, s], -(HD ** -0.5), head_cols(neg_sinks, i),
                                              ALU.mult, ALU.min))
                dve.tensor_tensor(sink_in[:, s], head_cols(sinks, i), neg_max[:, s], ALU.add).then_inc(max_ready, 1)

            def weigh(i):
                t, h0, n = STEPS[i]
                nk = (t + 1) * P
                s = slice(4 * (i % 2), 4 * (i % 2) + n)
                dve.wait_ge(exped, i + 1)
                step(dve.tensor_tensor(denom[:, 0:n], sums[:, s], sink_exp[:, s], ALU.add))
                step(dve.reciprocal(recip[:, s], denom[:, 0:n]))
                sc = probs[:, i % 2, :].rearrange("p (h k) -> p h k", h=n)
                dve.tensor_tensor(sc, sc, recip[:, s].unsqueeze(2).to_broadcast([P, n, nk]),
                                  ALU.mult).then_inc(weighted, 1)

            for i in range(NS + 1):
                if i < NS:
                    maxima_of(i)
                if i >= 1:
                    weigh(i - 1)
            for b in range(4):
                dve.wait_ge(ot_hi_ready, b + 1)
                dve.tensor_tensor(ot_lo[:, 2 * b:2 * b + 2, :].rearrange("p d t -> p (d t)"), banks[4 + b][:],
                                  ot_hi[:, 2 * b:2 * b + 2, :].bitcast(F32).rearrange("p d t -> p (d t)"),
                                  ALU.subtract).then_inc(ot_lo_ready, 1)
            split(U_O + 3)
            dve.wait_ge(unit_used, U_O + 4)
            dve.wait_ge(bo_added, NT)
            for t in range(NT):
                for half in range(2):
                    s = slice(half * CW, (half + 1) * CW)
                    mm = dve.tensor_tensor(x_res[:, t, s], x_res[:, t, s], banks[PROJ[t][half]][:], ALU.add)
                mm.then_inc(x_ready, 1)

            dve.wait_ge(x_ready, 3 * NT)
            norm(3)
            dve.wait_ge(gn_in, 16)
            for t in range(NT):
                dve.scalar_tensor_tensor(xn[:, t, :], x_res[:, t, :], rstd[:, t:t + 1], row_bc[:],
                                         ALU.mult, ALU.mult).then_inc(gained, 1)
            dve.wait_ge(gained, NT)
            for t in range(NT):
                dve.wait_ge(xs_hi_ready, t + 1)
                dve.tensor_tensor(xs_lo[:, t, :], xn[:, t, :], xs_hi[:, t, :].bitcast(F32),
                                  ALU.subtract).then_inc(xs_lo_ready, 1)
            dve.wait_ge(routed, 1)
            step(dve.tensor_copy(logits[:], banks[4][:, 0:NT * E]))
            for t in range(NT):
                step(dve.max(top[:, t * 8:t * 8 + 8], logits[:, t * E:(t + 1) * E]))
            tops = view3(top, NT)
            dve.tensor_tensor(gate_w[:, 0:2], tops[:, :, 1], tops[:, :, 0], ALU.subtract).then_inc(gate_in, 1)
            for t in range(NT):
                s = slice(t * E, (t + 1) * E)
                for rank, (of, to) in enumerate(((logits, first), (rest, second))):
                    step(dve.tensor_scalar(eq[:, s], of[:, s], top[:, t * 8 + rank:t * 8 + rank + 1], None, ALU.is_equal))
                    step(dve.tensor_tensor_scan(run[:, s], eq[:, s], zeros8[:], 0.0, ALU.add, ALU.add))
                    step(dve.scalar_tensor_tensor(to[:, s], run[:, s], 1.0, eq[:, s], ALU.is_equal, ALU.mult))
                    if rank == 0:
                        step(dve.scalar_tensor_tensor(rest[:, s], first[:, s], -3e38, logits[:, s], ALU.mult, ALU.add))
            dve.tensor_tensor(chosen[:], first[:], second[:], ALU.add).then_inc(chosen_ready, 1)
            dve.wait_ge(gate_exp, 1)
            step(dve.tensor_scalar(gate_w[:, 0:2], gate_w[:, 2:4], 1.0, None, ALU.add))
            step(dve.reciprocal(gate_w[:, 0:2], gate_w[:, 0:2]))
            step(dve.tensor_tensor(gate_w[:, 2:4], gate_w[:, 2:4], gate_w[:, 0:2], ALU.mult))
            for t in range(NT):
                s = slice(t * E, (t + 1) * E)
                step(dve.tensor_scalar(eq[:, s], first[:, s], gate_w[:, t:t + 1], None, ALU.mult))
                step(dve.scalar_tensor_tensor(comb3[:, t, 1:E + 1], second[:, s], gate_w[:, 2 + t:3 + t], eq[:, s],
                                              ALU.mult, ALU.add))
            dve.wait_ge(counted, 1)
            step(dve.tensor_tensor(run[:], banks[5][:, 0:NT * E], chosen[:], ALU.mult))
            step(dve.tensor_scalar(pos4[:, 0, :, 0:E], view3(run, NT), -1.0, None, ALU.add))
            step(dve.tensor_scalar(pos4[:, 1, :, :], pos4[:, 0, :, :], -float(P), None, ALU.add))
            step(dve.tensor_reduce(over[:, 0:1], banks[5][:, 2 * E:3 * E], AX_X, ALU.max))
            dve.tensor_scalar(over_flag[:], over[:, 0:1], float(P), None, ALU.is_gt).then_inc(flag_ready, 1)

            def expert_pass(ps):
                if ps.x0:
                    dve.wait_ge(pick_turned, ps.p0)
                    dve.wait_ge(gathered, ps.x0)
                pick_tokens(ps, slice(0, 1), 0)
                take_gathered(2 * ps.x0)
                with dve.Fori(0, E) as e:
                    feed_forward(ps, e)
                take_output(2 * (ps.x0 + E))
                dve.wait_ge(added, 2 * (ps.x0 + E))
                add_scattered(ps, slice(E, E + 1), 2 * (ps.x0 + E))
                dve.wait_ge(added, 2 * (ps.x0 + E + 1))

            expert_pass(PASSES[1])
            dve.wait_ge(flag_ready, 1)
            again = dve.value_load(over_flag[0:1, 0:1], min_val=0, max_val=1)
            with dve.If(again > 0):
                expert_pass(PASSES[2])

            dve.memset(var[:], 0.0).then_inc(stream_done, 1)
            norm(4)
            dve.wait_ge(gf_in, 16)
            for t in range(NT):
                dve.scalar_tensor_tensor(xn[:, t, :], x_res[:, t, :], rstd[:, t:t + 1], row_bc[:],
                                         ALU.mult, ALU.mult).then_inc(xn_ready, 1)


_INS = ["x", "norm_mix", "norm_ffn", "pool_w", "pool_b", "pool_scale", "norm_kv", "w_kv", "b_kv", "w_q", "b_q",
        "attn_sinks", "w_o", "b_o", "ffn_w1", "ffn_w3", "ffn_w2", "router_w", "moe_w1", "moe_w3", "moe_w2",
        "norm_final"]


def kernel(**inputs):
    import concourse.bacc as bacc
    from concourse.bass_utils import run_bass_kernel_spmd

    table, bands = shape_constants()
    nc = bacc.Bacc("TRN2", target_bir_lowering=False, num_devices=1)
    arrays = {f"in_{name}": np.ascontiguousarray(inputs[name]) for name in _INS}
    arrays["in_table"] = table
    arrays["in_bands"] = bands
    args = [nc.dram_tensor(name, a.shape, mybir.dt.from_np(a.dtype), kind="ExternalInput").ap()
            for name, a in arrays.items()]
    out = nc.dram_tensor("out_x", (1, SEQ, D), F32, kind="ExternalOutput").ap()
    trunk_program(nc, *args, out)
    result = run_bass_kernel_spmd(nc, [arrays], core_ids=[0])
    return result.results[0]["out_x"]
```

```python
import numpy as np
from contextlib import ExitStack

import concourse.bass as bass
from concourse import mybir

F32 = mybir.dt.float32
F32R = mybir.dt.float32r
I32 = mybir.dt.int32
ALU = mybir.AluOpType
ACT = mybir.ActivationFunctionType
AX_X = mybir.AxisListType.X

P = 128
SEQ = 256
D = 1024
F = 3584
E = 8
HD = 64
NH = 16
CHUNK = 64
WINDOWS = (2, 4, 8, 16)
NT = SEQ // P
NPAIR = NH // 2
DT = D // P
CW = 512
NC = F // CW
UNIT = 2048
RING = 14
NHI = 3
EPS = 1e-5

FFN_UNITS = []
for _c in range(NC + 1):
    if _c < NC:
        FFN_UNITS += [("w1", _c, 0), ("w1", _c, 1), ("w3", _c, 0), ("w3", _c, 1)]
    if _c > 0:
        FFN_UNITS += [("w2", _c - 1, 0), ("w2", _c - 1, 1)]
NU = len(FFN_UNITS)
AT = {key: j for j, key in enumerate(FFN_UNITS)}
TURN = {c: AT[("w2", c - 1, 0)] if c else AT[("w1", 1, 1)] for c in range(NC)}
SCATTER_AT = AT[("w3", 0, 1)]
GATHER_AT = AT[("w2", NC - 2, 1)]
PICK_AT = AT[("w3", 2, 0)]

U_BAND, U_POOLW = 0, 1
U_DENSE = 2
U_KV = U_DENSE + NU
U_Q = U_KV + 1
U_O = U_Q + 4
U_MOE = (U_O + 4, U_O + 4 + E * NU)
assert NU % RING == 0 and NU % NHI == 0

C_ID, C_TRI, C_ONE, C_IOTA = 0, P, 2 * P, 3 * P
C_COS, C_SIN = 4 * P, 6 * P
C_N = 8 * P


def shape_constants():
    t = np.arange(SEQ)
    table = np.zeros((P, C_N), np.float32)
    table[:, C_ID:C_ID + P] = np.eye(P)
    table[:, C_TRI:C_TRI + P] = np.triu(np.ones((P, P)))
    table[:, C_ONE:C_ONE + P] = 1.0
    table[:, C_IOTA:C_IOTA + P] = np.arange(P)[None, :]
    half = HD // 2
    inv = (np.float32(10000.0) ** (-np.arange(half, dtype=np.float32) / half)).astype(np.float32)
    ang = t.astype(np.float32)[None, :] * inv[:, None]
    row = np.arange(P) % half
    table[:, C_COS:C_COS + SEQ] = np.cos(ang)[row]
    sign = np.where(np.arange(P) % HD < half, 1.0, -1.0)[:, None]
    table[:, C_SIN:C_SIN + SEQ] = np.sin(ang)[row] * sign
    bands = np.zeros((len(WINDOWS), SEQ, SEQ), np.float32)
    for g, win in enumerate(WINDOWS):
        back = t[None, :] - t[:, None]
        mean = ((back >= 0) & (back < win)) / np.minimum(t + 1, win)[None, :].astype(np.float32)
        bands[g] = mean.astype(np.float32) - np.eye(SEQ, dtype=np.float32)
    bands = bands.reshape(len(WINDOWS), NT, P, SEQ).transpose(2, 0, 1, 3)
    return table, np.ascontiguousarray(bands.reshape(P, -1))


def trunk_program(nc, x, norm_mix, norm_ffn, pool_w, pool_b, pool_scale, norm_kv, w_kv, b_kv, w_q, b_q,
                  attn_sinks, w_o, b_o, ffn_w1, ffn_w3, ffn_w2, router_w, moe_w1, moe_w3, moe_w2,
                  norm_final, table, bands, out):
    ctx = ExitStack()
    with ctx:
        K = 1024
        arena_bytes = (RING + NHI) * UNIT * 4 + 64 * K + P * 4 + C_N * 4 + 2 * K
        arena = ctx.enter_context(nc.sbuf_tensor("arena", [P, arena_bytes // 4], F32))
        base = nc.sbuf_base - arena_bytes
        end = [base]

        def at(name, shape, dtype, offset):
            return nc.alloc_sbuf_tensor_at(name, shape, dtype, offset=offset)

        def place(nbytes):
            end[0] += nbytes
            assert end[0] <= base + arena_bytes
            return end[0] - nbytes

        o_raw = place(RING * UNIT * 4)
        raw = [at(f"raw{r}", [P, UNIT], F32, o_raw + r * UNIT * 4) for r in range(RING)]
        low = [at(f"low{r}", [P, UNIT], F32R, o_raw + r * UNIT * 4) for r in range(RING)]
        high = [at(f"high{r}", [P, UNIT], F32R, place(UNIT * 4)) for r in range(NHI)]
        x_res = at("x_res", [P, NT, D], F32, place(8 * K))
        o_a = place(16 * K)
        o_b = place(16 * K)
        o_w = place(20 * K)
        row_bc = at("row_bc", [P, D], F32, place(4 * K))
        consts = at("consts", [P, C_N], F32, place(C_N * 4))
        b_v = at("b_v", [P, P], F32, place(P * 4))
        o_s = place(2 * K)

        a_hi = at("a_hi", [P, DT, SEQ], F32R, o_a)
        a_lo = at("a_lo", [P, DT, SEQ], F32R, o_a + 8 * K)
        xg_hi = at("xg_hi", [P, DT, P], F32R, o_a)
        xg_lo = at("xg_lo", [P, DT, P], F32R, o_a + 8 * K)
        probs = at("probs", [P, 2, CW], F32, o_a)
        probs_t = at("probs_t", [P, 2, CW], F32, o_a + 8 * K)
        b_hi = at("b_hi", [P, 2, NT, CW], F32R, o_b)
        b_lo = at("b_lo", [P, 2, NT, CW], F32R, o_b + 8 * K)
        pool_rows = at("pool_rows", [P, 2, D], F32, o_b)
        pool_bs = at("pool_bs", [P, D], F32, o_b + 8 * K)
        pool_y = at("pool_y", [P, D], F32, o_b + 12 * K)
        kv_hi = b_hi[:].rearrange("p a b c -> p (a b c)").rearrange("p (d t) -> p d t", d=DT)
        kv_lo = b_lo[:].rearrange("p a b c -> p (a b c)").rearrange("p (d t) -> p d t", d=DT)
        ot_hi, ot_lo = kv_hi, kv_lo
        xs_hi = b_hi[:].rearrange("p a b c -> p (a b c)").rearrange("p (t d) -> p t d", t=NT)
        xs_lo = b_lo[:].rearrange("p a b c -> p (a b c)").rearrange("p (t d) -> p t d", t=NT)
        pooled_t = at("pooled_t", [P, DT, SEQ], F32, o_w)
        xn_t = at("xn_t", [P, DT, SEQ], F32, o_w)
        q_t = at("q_t", [P, NH // 4, SEQ // CHUNK, 2 * CHUNK], F32, o_w)
        h_t = at("h_t", [P, DT, SEQ], F32, o_w)
        xn = at("xn", [P, NT, D], F32, o_w + 8 * K)
        rope_x = at("rope_x", [P, 2, 2, SEQ], F32, o_w + 8 * K)
        rope_y = at("rope_y", [P, 2, SEQ], F32, o_w + 12 * K)
        rope_z = at("rope_z", [P, 2, SEQ], F32, o_w + 14 * K)
        hidden = at("hidden", [P, NT, CW], F32, o_w + 16 * K)
        k_t = at("k_t", [P, 2, SEQ], F32, o_w + 16 * K)
        v_win = at("v_win", [P, SEQ // CHUNK, P], F32, o_w + 18 * K)
        hm_hi = at("hm_hi", [P, 2, CW], F32R, o_w)
        hm_lo = at("hm_lo", [P, 2, CW], F32R, o_w + 4 * K)
        y_hi = at("y_hi", [P, D], F32R, o_w + 8 * K)
        y_lo = at("y_lo", [P, D], F32R, o_w + 12 * K)
        pick = at("pick", [P, NT, P], F32R, o_w + 18 * K)
        pick_t = at("pick_t", [P, SEQ], F32R, o_w + 19 * K)
        smalls = at("smalls", [P, 512], F32, o_s)
        small_at = [0]

        def small(n):
            small_at[0] += n
            assert small_at[0] <= 512
            return smalls[:, small_at[0] - n:small_at[0]]

        NV = 5 * DT + 1
        gains = small(NV)
        sinks = small(NPAIR)
        neg_sinks = small(NPAIR)
        sink_row = small(NH)
        sumsq = small(NT)
        var = small(NT)
        std = small(NT)
        rstd = small(NT)
        maxima = small(2 * NPAIR)
        neg_max = small(2 * NPAIR)
        sums = small(2 * NPAIR)
        sink_in = small(2 * NPAIR)
        sink_exp = small(2 * NPAIR)
        denom = small(NPAIR)
        recip = small(2 * NPAIR)
        r_w = small(DT * E)
        logits = small(NT * E)
        top = small(NT * 8)
        eq = small(NT * E)
        run = small(NT * E)
        first = small(NT * E)
        second = small(NT * E)
        rest = small(NT * E)
        chosen = small(NT * E)
        gate_w = small(NT * 4)
        position = small(2 * NT * (E + 1))
        combine = small(NT * (E + 1))
        first_key = small(E)
        warm_in = small(1)
        warm_out = small(1)
        best = small(NT)
        over = small(2)
        over_flag = small(1).bitcast(I32)
        vec_rows = at("vec_rows", [NV, P], F32, o_a)

        banks = [ctx.enter_context(nc.psum_tensor(f"bank{i}", [P, CW], F32)) for i in range(8)]
        UP1, UP3 = (0, 1), (2, 3)
        OUT = ((4, 5), (6, 7))
        TURN_BANK, PICK_BANK, GATHER = 1, 3, (6, 7)
        PROJ = ((0, 1), (2, 3))

        def view3(t, n):
            return t[:].rearrange("p (a b) -> p a b", a=n)

        ident = consts[:, C_ID:C_ID + P]
        pos4 = position[:].rearrange("p (s t e) -> p s t e", s=2, t=NT)
        comb3 = view3(combine, NT)

        def sem(name):
            return ctx.enter_context(nc.semaphore(name))

        landed = [sem(f"landed{r}") for r in range(RING)]
        split_hi, split_lo = sem("split_hi"), sem("split_lo")
        unit_used = sem("unit_used")
        x_in = [sem(f"x_in{t}") for t in range(NT)]
        consts_in, vec_in, pool_in = sem("consts_in"), sem("vec_in"), sem("pool_in")
        misc_in, bo_in, bv_in = sem("misc_in"), sem("bo_in"), sem("bv_in")
        gn_in, gf_in, out_done = sem("gn_in"), sem("gf_in"), sem("out_done")
        sumsq_ready, var_ready, std_ready = sem("sumsq_ready"), sem("var_ready"), sem("std_ready")
        xn_ready = sem("xn_ready")
        x_ready = sem("x_ready")
        stream_done = sem("stream_done")
        vec_turned, gains_ready = sem("vec_turned"), sem("gains_ready")
        pool_ready, pooled, pooled_out, mixed = sem("pool_ready"), sem("pooled"), sem("pooled_out"), sem("mixed")
        turned, a_hi_ready, a_lo_ready = sem("turned"), sem("a_hi_ready"), sem("a_lo_ready")
        activated, gated, hidden_turned = sem("activated"), sem("gated"), sem("hidden_turned")
        hidden_hi, hidden_lo = sem("hidden_hi"), sem("hidden_lo")
        xn_t_ready = sem("xn_t_ready")
        kv_hi_ready, kv_lo_ready, kv_done, v_out = sem("kv_hi_ready"), sem("kv_lo_ready"), sem("kv_done"), sem("v_out")
        biased, cosined, roped = sem("biased"), sem("cosined"), sem("roped")
        scored, half_scored, max_ready, exped = sem("scored"), sem("half_scored"), sem("max_ready"), sem("exped")
        weighted, probs_turned, probs_out, attended = sem("weighted"), sem("probs_turned"), sem("probs_out"), sem("attended")
        ot_hi_ready, ot_lo_ready, bo_added = sem("ot_hi_ready"), sem("ot_lo_ready"), sem("bo_added")
        gained, xs_hi_ready, xs_lo_ready = sem("gained"), sem("xs_hi_ready"), sem("xs_lo_ready")
        h_out, routed, gate_in, gate_exp = sem("h_out"), sem("routed"), sem("gate_in"), sem("gate_exp")
        chosen_ready, counted, flag_ready = sem("chosen_ready"), sem("counted"), sem("flag_ready")
        picked, gathered = sem("picked"), sem("gathered")
        xg_hi_ready, xg_lo_ready = sem("xg_hi_ready"), sem("xg_lo_ready")
        pick_turned, pick_t_ready = sem("pick_turned"), sem("pick_t_ready")
        y_hi_ready, y_lo_ready = sem("y_hi_ready"), sem("y_lo_ready")
        scattered, added = sem("scattered"), sem("added")
        dve_step, pool_step = sem("dve_step"), sem("pool_step")

        x_d = x.rearrange("o (t p) d -> p (o t) d", p=P)
        out_d = out.rearrange("o (t p) d -> p (o t) d", p=P)

        def up_view(w):
            return w.rearrange("o (k p) f -> o p k f", p=P)

        dense = {"w1": up_view(ffn_w1), "w3": up_view(ffn_w3), "w2": up_view(ffn_w2)}
        experts = {n: w.rearrange("o e (k p) f -> (o e) p k f", p=P)
                   for n, w in (("w1", moe_w1), ("w3", moe_w3), ("w2", moe_w2))}

        def bc(row):
            return row.rearrange("(o n) -> o n", o=1).to_broadcast([P, row.shape[0]])

        def ffn_source(views, e, kind, c, half):
            if kind == "w2":
                part = views[kind][bass.ds(e, 1), :, 4 * c + 2 * half:4 * c + 2 * half + 2, :]
            else:
                part = views[kind][bass.ds(e, 1), :, 4 * half:4 * half + 4, c * CW:(c + 1) * CW]
            return part.rearrange("o p k f -> p (o k) f")

        def slot(u):
            return u % RING

        def turn_bank(ps, c, t):
            return banks[TURN_BANK if ps.moe else OUT[0][t] if c == 0 else UP1[t]]

        def hslot(u):
            return (u - U_DENSE) % NHI

        def turned_x(d):
            return banks[d // 2][:, (d % 2) * SEQ:(d % 2 + 1) * SEQ]

        def raw3(u, k):
            return raw[slot(u)][:].rearrange("p (k f) -> p k f", k=k)

        def hi3(u, k):
            return high[hslot(u)][:].rearrange("p (k f) -> p k f", k=k)

        def lo3(u, k):
            return low[slot(u)][:].rearrange("p (k f) -> p k f", k=k)

        class Pass:

            def __init__(self, n):
                self.moe = n > 0
                self.tiles = 1 if n else NT
                self.block = n - 1
                self.u0 = U_MOE[n - 1] if n else U_DENSE
                self.k0 = NC + (n - 1) * E * NC if n else 0
                self.x0 = (n - 1) * (E + 1)
                self.p0 = (n - 1) * E

            def units(self, j, e):
                return e * NU + (self.u0 + j) if self.moe else self.u0 + j

            def chunks(self, c, e):
                return e * NC + (self.k0 + c) if self.moe else self.k0 + c

        PASSES = [Pass(0), Pass(1), Pass(2)]

        STEPS = ([(c, 0, 4, 2 * CHUNK) for c in (1, 2, 3)] + [(0, 0, NPAIR, CHUNK)]
                 + [(c, 4, 4, 2 * CHUNK) for c in (1, 2, 3)])
        NS = len(STEPS)

        def pair(j):
            return j // 4 * 2 + j % 2, j // 2 % 2

        def stat(t_, i):
            return t_[:, NPAIR * (i % 2):NPAIR * (i % 2) + STEPS[i][2]]

        ROPE = [(1, 4, 5 * DT)] + [(2, 6 + m % 2, 4 * DT + 2 * m) for m in range(4)]

        block = ctx.enter_context(nc.Block())

        @block.sync
        def _(sp):
            def load(u, src, k, used=None):
                used = u - RING + 1 if used is None else used
                if not isinstance(used, int) or used > 0:
                    sp.wait_ge(unit_used, used)
                sp.dma_start(raw3(u, k), src).then_inc(landed[slot(u)], 16)

            for t in range(NT):
                sp.dma_start(x_res[:, t, :], x_d[:, t, :]).then_inc(x_in[t], 16)
            load(U_BAND, bands.rearrange("p (k f) -> p k f", k=8), 8)
            load(U_POOLW, pool_w.rearrange("o g (k p) f -> p (o g k) f", p=P), 8)
            sp.wait_ge(vec_in, 16 * 6)
            sp.wait_ge(pool_in, 32)
            for j, key in enumerate(FFN_UNITS):
                load(U_DENSE + j, ffn_source(dense, 0, *key), 2 if key[0] == "w2" else 4)
            load(U_KV, w_kv.rearrange("(k p) f -> p k f", p=P), DT)
            for m in range(4):
                load(U_Q + m, w_q[0].rearrange("(k p) f -> p k f", p=P)[:, :, m * SEQ:(m + 1) * SEQ], DT)
            for m in range(4):
                load(U_O + m, w_o[0].rearrange("(k p) f -> p k f", p=P)[:, 2 * m:2 * m + 2, :], 2)

            def expert_loads(ps):
                with sp.Fori(0, E) as e:
                    for j, key in enumerate(FFN_UNITS):
                        load(ps.u0 + j, ffn_source(experts, e, *key), 2 if key[0] == "w2" else 4,
                             ps.units(j - RING + 1, e))

            expert_loads(PASSES[1])
            sp.wait_ge(flag_ready, 1)
            again = sp.value_load(over_flag[0:1, 0:1], min_val=0, max_val=1)
            with sp.If(again > 0):
                expert_loads(PASSES[2])
            for t in range(NT):
                sp.wait_ge(xn_ready, 3 * NT + t + 1)
                sp.dma_start(out_d[:, t, :], xn[:, t, :]).then_inc(out_done, 16)
            sp.wait_ge(out_done, 16 * NT)

        @block.gpsimd
        def _(pool):
            pool.wait_ge(pool_in, 32)
            pool.tensor_tensor(pool_bs[:], pool_rows[:, 0, :], pool_rows[:, 1, :], ALU.mult).then_inc(pool_step, 1)
            pool.wait_ge(pool_step, 1)
            pool.wait_ge(xn_ready, NT)
            for t in range(NT):
                pool.tensor_tensor(x_res[:, t, :], x_res[:, t, :], pool_bs[:], ALU.add).then_inc(pool_ready, 1)
            pool.wait_ge(xn_ready, 3 * NT)
            pool.dma_start(b_v[:], bc(b_kv[P:2 * P])).then_inc(bv_in, 16)
            pool.wait_ge(bo_in, 16)
            for t in range(NT):
                pool.tensor_tensor(x_res[:, t, :], x_res[:, t, :], row_bc[:], ALU.add).then_inc(bo_added, 1)
            for i, (n, _, _) in enumerate(ROPE):
                pool.wait_ge(biased, i + 1)
                if i:
                    pool.wait_ge(roped, i)
                pool.tensor_tensor(rope_y[:, 0:n, :], rope_x[:, i % 2, 0:n, :],
                                   consts[:, C_COS:C_COS + SEQ].unsqueeze(1).to_broadcast([P, n, SEQ]),
                                   ALU.mult).then_inc(cosined, 1)
            pool.wait_ge(bo_added, NT)
            pool.dma_start(row_bc[:], bc(norm_ffn[1])).then_inc(gn_in, 16)
            pool.wait_ge(gained, NT)
            pool.dma_start(row_bc[:], bc(norm_final)).then_inc(gf_in, 16)
            pool.memset(pick_t[:].bitcast(F32), 0.0).then_inc(pick_t_ready, 1)

        @block.tensor
        def _(pe):
            def three_passes(o, s_hi, s_lo, m_hi, m_lo, start, stop):
                pe.matmul(o, s_hi, m_hi, start=start, stop=False)
                pe.matmul(o, s_lo, m_hi, start=False, stop=False)
                return pe.matmul(o, s_hi, m_lo, start=False, stop=stop)

            def keep_warm(bank, n):
                for _ in range(n):
                    pe.matmul(banks[bank][:, 0:P], ident, ident, start=True, stop=True)

            def turn_stream():
                for d in range(DT):
                    for t in range(NT):
                        at_ = (d % 2) * SEQ + t * P
                        mm = pe.transpose(banks[d // 2][:, at_:at_ + P], xn[:, t, d * P:(d + 1) * P], ident)
                    if d % 2:
                        mm.then_inc(turned, 1)

            def gather():
                for d in range(DT):
                    o = banks[GATHER[d // 4]][:, (d % 4) * P:(d % 4 + 1) * P]
                    for t in range(NT):
                        pe.matmul(o, xs_hi[:, t, d * P:(d + 1) * P], pick[:, t, :], start=t == 0, stop=False)
                        mm = pe.matmul(o, xs_lo[:, t, d * P:(d + 1) * P], pick[:, t, :],
                                       start=False, stop=t == NT - 1)
                mm.then_inc(gathered, 1)

            def scatter():
                for t, pair in enumerate((OUT[0], GATHER)):
                    s = pick_t[:, t * P:(t + 1) * P]
                    for half in range(2):
                        m = slice(half * CW, (half + 1) * CW)
                        pe.matmul(banks[pair[half]][:], s, y_hi[:, m], start=True, stop=False)
                        mm = pe.matmul(banks[pair[half]][:], s, y_lo[:, m], start=False, stop=True)
                    mm.then_inc(scattered, 1)

            def feed_forward(ps, e):
                act_hi, act_lo = (xg_hi, xg_lo) if ps.moe else (a_hi, a_lo)
                for j, (kind, c, half) in enumerate(FFN_UNITS):
                    u = ps.u0 + j
                    pe.wait_ge(split_lo, ps.units(j - U_DENSE + 1, e))
                    if half == 0 and kind == "w1":
                        if ps.moe or c == 1:
                            pe.wait_ge(activated, ps.chunks(c, e))
                        elif c:
                            pe.wait_ge(hidden_lo, ps.chunks(c, e))
                        if c == 0 and ps.moe:
                            pe.wait_ge(xg_lo_ready, e + (ps.p0 + 1))
                    if half == 0 and kind == "w3" and (ps.moe or c):
                        pe.wait_ge(gated, ps.chunks(c, e))
                    if kind == "w2" and half == 0:
                        pe.wait_ge(hidden_lo, ps.chunks(c + 1, e))
                        if c == 0 and ps.moe:
                            pe.wait_ge(added, e * 2 + (2 * ps.x0 + 1))
                    if kind == "w2":
                        for ft in range(2):
                            i = 2 * half + ft
                            s = slice(i * P, (i + 1) * P)
                            for t in range(ps.tiles):
                                s_hi = hm_hi[:, c % 2, s] if ps.moe else b_hi[:, c % 2, t, s]
                                s_lo = hm_lo[:, c % 2, s] if ps.moe else b_lo[:, c % 2, t, s]
                                for nh in range(2):
                                    m = slice(nh * CW, (nh + 1) * CW)
                                    mm = three_passes(banks[OUT[t][nh]][:], s_hi, s_lo,
                                                      hi3(u, 2)[:, ft, m], lo3(u, 2)[:, ft, m],
                                                      c == 0 and i == 0, c == NC - 1 and i == 3)
                    else:
                        up = UP1 if kind == "w1" else UP3
                        for k in range(4):
                            d = 4 * half + k
                            if kind == "w1" and c == 0 and not ps.moe:
                                pe.wait_ge(a_lo_ready, max(d + 1, 4))
                            for t in range(ps.tiles):
                                s = slice(t * P, (t + 1) * P)
                                mm = three_passes(banks[up[t]][:], act_hi[:, d, s], act_lo[:, d, s],
                                                  hi3(u, 4)[:, k, :], lo3(u, 4)[:, k, :], d == 0, d == DT - 1)
                    mm.then_inc(unit_used, 1)
                    if ps.moe and j == SCATTER_AT:
                        pe.wait_ge(y_lo_ready, e + (ps.x0 + 1))
                        pe.wait_ge(pick_t_ready, e + (ps.p0 + 1))
                        scatter()
                        for t in range(NT):
                            mm = pe.transpose(banks[PICK_BANK][:, t * P:(t + 1) * P],
                                              pick[:, t, :].bitcast(F32), ident)
                        mm.then_inc(pick_turned, 1)
                    for cc in range(NC):
                        if TURN[cc] == j:
                            pe.wait_ge(gated, ps.chunks(cc + 1, e))
                            for t in range(ps.tiles):
                                for i in range(4):
                                    mm = pe.transpose(turn_bank(ps, cc, t)[:, i * P:(i + 1) * P],
                                                      hidden[:, t, i * P:(i + 1) * P], ident)
                            mm.then_inc(hidden_turned, 1)
                    if ps.moe and j == GATHER_AT:
                        pe.wait_ge(picked, e + (ps.x0 + 2))
                        pe.wait_ge(added, e * 2 + (2 * ps.x0 + 2))
                        gather()

            pe.wait_ge(consts_in, 16)
            pe.wait_ge(vec_in, 16 * 6)
            pe.transpose(banks[7][:, 0:NV], vec_rows[:, :], ident[0:NV, 0:NV]).then_inc(vec_turned, 1)

            pe.wait_ge(xn_ready, NT)
            pe.wait_ge(landed[U_BAND], 16)
            band = raw3(U_BAND, 8)
            reach = max(WINDOWS)
            for d in range(DT):
                o, s, g = banks[d // 2], slice(d * P, (d + 1) * P), d // 2
                at_ = (d % 2) * SEQ
                pe.matmul(o[:, at_ + P:at_ + SEQ], xn[:, 1, s], band[:, g * NT + 1, P:SEQ], start=True, stop=False)
                pe.matmul(o[:, at_ + P:at_ + P + reach], xn[:, 0, s], band[:, g * NT, P:P + reach],
                          start=False, stop=False)
                mm = pe.matmul(o[:, at_:at_ + P], xn[:, 0, s], band[:, g * NT, 0:P], start=False, stop=True)
                if d % 2:
                    mm.then_inc(pooled, 1)
            pe.wait_ge(pooled, DT // 2)
            pe.wait_ge(landed[U_POOLW], 16)
            pe.wait_ge(gains_ready, 1)
            w = raw3(U_POOLW, 8)
            for g in range(len(WINDOWS)):
                pe.wait_ge(pooled_out, g + 1)
                for t in range(NT):
                    for k in range(2):
                        mm = pe.matmul(banks[OUT[t][g // 2]][:, (g % 2) * SEQ:(g % 2 + 1) * SEQ],
                                       pooled_t[:, 2 * g + k, t * P:(t + 1) * P], w[:, 2 * g + k, :],
                                       start=k == 0, stop=k == 1)
                if g % 2:
                    mm.then_inc(mixed, 1)
            pe.wait_ge(mixed, 2)
            pe.nop().then_inc(unit_used, 2)

            keep_warm(0, 28)
            pe.wait_ge(xn_ready, 2 * NT)
            turn_stream()
            feed_forward(PASSES[0], 0)

            keep_warm(0, 30)
            pe.wait_ge(xn_ready, 3 * NT)
            turn_stream()
            pe.wait_ge(split_lo, U_KV - U_DENSE + 1)
            wh, wl = hi3(U_KV, DT), lo3(U_KV, DT)
            for d in range(DT):
                pe.wait_ge(kv_lo_ready, d + 1)
                mm = three_passes(banks[4][:, 0:SEQ], wh[:, d, 0:P], wl[:, d, 0:P], kv_hi[:, d, :], kv_lo[:, d, :],
                                  d == 0, d == DT - 1)
            mm.then_inc(kv_done, 1)
            for t in range(NT):
                s = slice(t * P, (t + 1) * P)
                for d in range(DT):
                    mm = three_passes(banks[5][:, s], kv_hi[:, d, s], kv_lo[:, d, s], wh[:, d, P:2 * P],
                                      wl[:, d, P:2 * P], d == 0, d == DT - 1)
            mm.then_inc(unit_used, 1)
            pe.wait_ge(a_lo_ready, 2 * DT)
            for m in range(4):
                u = U_Q + m
                pe.wait_ge(split_lo, u - U_DENSE + 1)
                if m >= 2:
                    pe.wait_ge(biased, m)
                for n in range(2):
                    for d in range(DT):
                        s = slice(n * P, (n + 1) * P)
                        mm = three_passes(banks[6 + m % 2][:, n * SEQ:(n + 1) * SEQ], hi3(u, DT)[:, d, s],
                                          lo3(u, DT)[:, d, s], a_hi[:, d, :], a_lo[:, d, :], d == 0, d == DT - 1)
                mm.then_inc(unit_used, 1)

            def scores(i):
                c, j0, n, nk = STEPS[i]
                k0 = max(c - 1, 0) * CHUNK
                if i >= 2:
                    pe.wait_ge(exped, i - 1)
                for k, a in enumerate(sorted(range(n), key=lambda a: pair(j0 + a)[1])):
                    b, r = pair(j0 + a)
                    if k == n // 2:
                        mm.then_inc(half_scored, 1)
                        pe.wait_ge(half_scored, i + 1)
                    rows = slice(HD * r, HD * r + HD)
                    mm = pe.matmul(banks[i % 2][:, a * nk:(a + 1) * nk],
                                   q_t[rows, b, c, :],
                                   k_t[rows, b // 2, k0:k0 + nk], start=True, stop=True)
                mm.then_inc(scored, 1)

            def turn_probs(i):
                pe.wait_ge(weighted, i + 1)
                if i >= 2:
                    pe.wait_ge(probs_out, i - 1)
                for a in range(4):
                    mm = pe.transpose(banks[2 + i % 2][:, a * P:(a + 1) * P], probs[:, i % 2, a * P:(a + 1) * P], ident)
                mm.then_inc(probs_turned, 1)

            def attend(i):
                c, j0, n, nk = STEPS[i]
                pe.wait_ge(probs_out, i + 1)
                for a in range(n):
                    b, r = pair(j0 + a)
                    keys = slice(a % 2 * CHUNK, (a % 2 + 1) * CHUNK) if c == 0 else slice(0, P)
                    at_ = (a // 2 if c == 0 else a) * P
                    o = banks[4 + b][HD * r:HD * r + HD, :].rearrange("p (a t) -> p a t", a=2)
                    mm = pe.matmul(o[:, :, c * CHUNK:(c + 1) * CHUNK], v_win[keys, c, b // 2 * HD:(b // 2 + 1) * HD],
                                   probs_t[keys, i % 2, at_:at_ + P].rearrange("p (a t) -> p a t", a=2),
                                   start=True, stop=True)
                mm.then_inc(attended, 1)

            pe.wait_ge(roped, len(ROPE))
            pe.wait_ge(v_out, 1)
            scores(0)
            for i in range(NS + 2):
                if i + 1 < NS:
                    scores(i + 1)
                if 1 <= i <= NS:
                    turn_probs(i - 1)
                if i >= 2:
                    attend(i - 2)

            pe.wait_ge(ot_lo_ready, 4)
            for m in range(4):
                u = U_O + m
                pe.wait_ge(split_lo, u - U_DENSE + 1)
                for k in range(2):
                    d = 2 * m + k
                    for t in range(NT):
                        s = slice(t * P, (t + 1) * P)
                        for nh in range(2):
                            c = slice(nh * CW, (nh + 1) * CW)
                            mm = three_passes(banks[PROJ[t][nh]][:], ot_hi[:, d, s], ot_lo[:, d, s],
                                              hi3(u, 2)[:, k, c], lo3(u, 2)[:, k, c], d == 0, d == DT - 1)
                mm.then_inc(unit_used, 1)

            keep_warm(7, 26)
            pe.wait_ge(gained, NT)
            turn_stream()
            keep_warm(7, 4)
            pe.wait_ge(h_out, DT // 2)
            pe.wait_ge(misc_in, 16 * 2)
            for t in range(NT):
                for d in range(DT):
                    mm = pe.matmul(banks[4][:, t * E:(t + 1) * E], h_t[:, d, t * P:(t + 1) * P],
                                   r_w[:, d * E:(d + 1) * E], start=d == 0, stop=d == DT - 1)
            mm.then_inc(routed, 1)
            keep_warm(7, 12)
            pe.wait_ge(chosen_ready, 1)
            tri, ones = consts[:, C_TRI:C_TRI + P], consts[:, C_ONE:C_ONE + P]
            c0, c1 = chosen[:, 0:E], chosen[:, E:2 * E]
            pe.matmul(banks[5][:, 0:E], tri, c0, start=True, stop=True)
            pe.matmul(banks[5][:, E:2 * E], tri, c1, start=True, stop=False)
            pe.matmul(banks[5][:, E:2 * E], ones, c0, start=False, stop=True)
            pe.matmul(banks[5][:, 2 * E:3 * E], ones, c0, start=True, stop=False)
            pe.matmul(banks[5][:, 2 * E:3 * E], ones, c1, start=False, stop=True).then_inc(counted, 1)

            def expert_pass(ps):
                if not ps.x0:
                    keep_warm(7, 5)
                pe.wait_ge(picked, ps.x0 + 1)
                pe.wait_ge(xs_lo_ready, NT)
                if ps.x0:
                    pe.wait_ge(added, 2 * ps.x0)
                gather()
                if not ps.x0:
                    keep_warm(0, 9)
                with pe.Fori(0, E) as e:
                    feed_forward(ps, e)
                pe.wait_ge(y_lo_ready, ps.x0 + E + 1)
                pe.wait_ge(pick_t_ready, ps.p0 + E + 1)
                scatter()

            expert_pass(PASSES[1])
            pe.wait_ge(flag_ready, 1)
            again = pe.value_load(over_flag[0:1, 0:1], min_val=0, max_val=1)
            with pe.If(again > 0):
                expert_pass(PASSES[2])

        @block.scalar
        def _(act):
            def split(u, ps=None, j=0, e=0):
                r = slot(u)
                if ps is not None and ps.moe:
                    act.wait_ge(landed[r], e * (16 * NU // RING) + 16 * (u // RING + 1))
                    act.wait_ge(unit_used, ps.units(j - NHI + 1, e))
                else:
                    act.wait_ge(landed[r], 16 * (u // RING + 1))
                    if u - NHI >= U_DENSE:
                        act.wait_ge(unit_used, u - NHI + 1)
                act.activation(high[hslot(u)][:], raw[r][:], ACT.Copy).then_inc(split_hi, 1)

            def warm(func):
                act.activation(warm_out, warm_in, func)

            def norm(n, ready):
                warm(ACT.Sqrt)
                for t in range(NT):
                    act.wait_ge(*ready(t))
                    act.activation(xn[:, t, :], x_res[:, t, :], ACT.Square,
                                   accum_out=sumsq[:, t:t + 1]).then_inc(sumsq_ready, 1)
                act.wait_ge(var_ready, n + 1)
                act.activation(std[:], var[:], ACT.Sqrt).then_inc(std_ready, 1)

            def gained_high(row, src, dst, signal, ready=None):
                for d in range(DT):
                    if ready is not None and d % 2 == 0:
                        act.wait_ge(ready, d // 2 + 1)
                    act.activation(dst[:, d, :], src(d), ACT.Copy,
                                   scale=gains[:, row * DT + d:row * DT + d + 1]).then_inc(signal, 1)

            def take_gathered(n):
                act.wait_ge(gathered, n)
                for half in range(2):
                    act.activation(xg_hi[:, 4 * half:4 * half + 4, :].rearrange("p d t -> p (d t)"),
                                   banks[GATHER[half]][:], ACT.Copy).then_inc(xg_hi_ready, 1)

            def take_output():
                for half in range(2):
                    act.activation(y_hi[:, half * CW:(half + 1) * CW], banks[OUT[0][half]][:],
                                   ACT.Copy).then_inc(y_hi_ready, 1)

            def feed_forward(ps, e, ahead=0):
                if ps.moe:
                    warm(ACT.Silu)
                for j, (kind, c, half) in enumerate(FFN_UNITS):
                    if ps.moe and j == 2:
                        act.wait_ge(unit_used, ps.units(0, e))
                        take_output()
                    for cc in range(NC):
                        if AT[("w1", cc, 1)] + NHI == j:
                            act.wait_ge(unit_used, ps.units(AT[("w1", cc, 1)] + 1, e))
                            if ps.moe or cc:
                                act.wait_ge(hidden_turned, ps.chunks(cc, e))
                            for t in range(ps.tiles):
                                mm = act.activation(hidden[:, t, :], banks[UP1[t]][:], ACT.Silu)
                            mm.then_inc(activated, 1)
                    if ps.moe and j == SCATTER_AT + NHI:
                        act.wait_ge(pick_turned, e + (ps.p0 + 1))
                        act.activation(pick_t[:], banks[PICK_BANK][:, 0:SEQ], ACT.Copy).then_inc(pick_t_ready, 1)
                    for cc in range(NC):
                        if TURN[cc] + NHI == j:
                            act.wait_ge(hidden_turned, ps.chunks(cc + 1, e))
                            for t in range(ps.tiles):
                                dst = hm_hi[:, cc % 2, :] if ps.moe else b_hi[:, cc % 2, t, :]
                                mm = act.activation(dst, turn_bank(ps, cc, t)[:], ACT.Copy)
                            mm.then_inc(hidden_hi, 1)
                    if j >= ahead:
                        split(ps.u0 + j, ps, j, e)
                    if ps.moe and j == 0:
                        take_gathered(e + (ps.x0 + 1))

            act.dma_start(consts[:], table).then_inc(consts_in, 16)
            for i, v in enumerate((norm_mix[0], norm_ffn[0], norm_kv, norm_mix[1], b_q[0])):
                act.dma_start(vec_rows[i * DT:(i + 1) * DT, :], v.rearrange("(d p) -> d p", p=P)).then_inc(vec_in, 16)
            act.dma_start(vec_rows[5 * DT:NV, :], b_kv[0:P].rearrange("(d p) -> d p", p=P)).then_inc(vec_in, 16)
            act.dma_start(pool_rows[:, 0, :], bc(pool_b.rearrange("o g d -> (o g d)"))).then_inc(pool_in, 16)
            act.dma_start(pool_rows[:, 1, :], bc(pool_scale[0])).then_inc(pool_in, 16)

            act.wait_ge(dve_step, 1)
            norm(0, lambda t: (x_in[t], 16))
            for i in range(NHI):
                split(U_DENSE + i)
            act.dma_start(row_bc[:], bc(b_o[0])).then_inc(bo_in, 16)
            act.dma_start(sink_row[:], bc(attn_sinks[0])).then_inc(misc_in, 16)
            act.dma_start(view3(r_w, DT), router_w[0].rearrange("(k p) e -> p k e", p=P)).then_inc(misc_in, 16)
            norm(1, lambda t: (x_ready, t + 1))
            warm(ACT.Silu)
            gained_high(1, turned_x, a_hi, a_hi_ready, turned)
            feed_forward(PASSES[0], 0, ahead=NHI)

            for i in range(NHI):
                split(U_KV + i)
            norm(2, lambda t: (x_ready, NT + t + 1))
            for b in range(4):
                act.wait_ge(turned, DT // 2 + b + 1)
                act.activation(xn_t[:, 2 * b:2 * b + 2, :].rearrange("p d t -> p (d t)"), banks[b][:],
                               ACT.Copy).then_inc(xn_t_ready, 1)
            act.wait_ge(xn_t_ready, 4)
            gained_high(2, lambda d: xn_t[:, d, :], kv_hi, kv_hi_ready)
            gained_high(3, lambda d: xn_t[:, d, :], a_hi, a_hi_ready)
            for i, (n, b, col) in enumerate(ROPE):
                if i:
                    act.wait_ge(unit_used, U_KV + 1 + i)
                else:
                    act.wait_ge(kv_done, 1)
                if i >= 2:
                    act.wait_ge(roped, i - 1)
                for k in range(n):
                    mm = act.activation(rope_x[:, i % 2, k, :], banks[b][:, k * SEQ:(k + 1) * SEQ], ACT.Identity,
                                        bias=gains[:, col + k:col + k + 1])
                mm.then_inc(biased, 1)
                if NHI + i < 5 + NHI:
                    split(U_KV + NHI + i)

            warm(ACT.Exp)

            def exponentials(i):
                c, j0, n, nk = STEPS[i]
                act.wait_ge(max_ready, i + 1)
                if i >= 2:
                    act.wait_ge(weighted, i - 1)
                    act.wait_ge(probs_turned, i - 1)
                for a in range(n):
                    keys = slice(a * nk, (a + 1) * nk)
                    act.activation(probs[:, i % 2, keys], banks[i % 2][:, keys], ACT.Exp,
                                   bias=stat(neg_max, i)[:, a:a + 1], scale=HD ** -0.5,
                                   accum_out=stat(sums, i)[:, a:a + 1])
                act.activation(stat(sink_exp, i), stat(sink_in, i), ACT.Exp).then_inc(exped, 1)

            def take_probs(i):
                act.wait_ge(probs_turned, i + 1)
                if i >= 2:
                    act.wait_ge(attended, i - 1)
                act.activation(probs_t[:, i % 2, :], banks[2 + i % 2][:], ACT.Copy).then_inc(probs_out, 1)

            for i in range(NS + 1):
                if i < NS:
                    exponentials(i)
                if i >= 1:
                    take_probs(i - 1)
            act.wait_ge(attended, NS)
            for b in range(4):
                act.activation(ot_hi[:, 2 * b:2 * b + 2, :].rearrange("p d t -> p (d t)"), banks[4 + b][:],
                               ACT.Copy).then_inc(ot_hi_ready, 1)
            split(U_O + 3)

            norm(3, lambda t: (x_ready, 2 * NT + t + 1))
            warm(ACT.Exp)
            for b in range(4):
                act.wait_ge(turned, (DT // 2) * 2 + b + 1)
                act.activation(h_t[:, 2 * b:2 * b + 2, :].rearrange("p d t -> p (d t)"), banks[b][:],
                               ACT.Copy).then_inc(h_out, 1)
            for t in range(NT):
                act.wait_ge(gained, t + 1)
                act.activation(xs_hi[:, t, :], xn[:, t, :], ACT.Copy).then_inc(xs_hi_ready, 1)
            act.wait_ge(gate_in, 1)
            act.activation(gate_w[:, 2:4], gate_w[:, 0:2], ACT.Exp).then_inc(gate_exp, 1)

            def expert_pass(ps):
                with act.Fori(0, E) as e:
                    feed_forward(ps, e)
                act.wait_ge(unit_used, ps.u0 + E * NU)
                take_output()

            act.wait_ge(flag_ready, 1)
            expert_pass(PASSES[1])
            again = act.value_load(over_flag[0:1, 0:1], min_val=0, max_val=1)
            with act.If(again > 0):
                expert_pass(PASSES[2])

            norm(4, lambda t: (stream_done, 1))

        @block.vector
        def _(dve):
            steps = [0]

            def step(instruction):
                steps[0] += 1
                instruction.then_inc(dve_step, 1)
                dve.wait_ge(dve_step, steps[0])

            def split(u, ps=None, j=0, e=0):
                dve.wait_ge(split_hi, ps.units(j - U_DENSE + 1, e) if ps else u - U_DENSE + 1)
                dve.tensor_tensor(low[slot(u)][:], raw[slot(u)][:], high[hslot(u)][:].bitcast(F32),
                                  ALU.subtract).then_inc(split_lo, 1)

            def norm(n):
                dve.wait_ge(sumsq_ready, NT * (n + 1))
                dve.tensor_scalar(var[:], sumsq[:], 1.0 / D, EPS, ALU.mult, ALU.add).then_inc(var_ready, 1)
                dve.wait_ge(std_ready, n + 1)
                step(dve.reciprocal(rstd[:], std[:]))

            def normalise(n):
                norm(n)
                for t in range(NT):
                    dve.tensor_scalar(xn[:, t, :], x_res[:, t, :], rstd[:, t:t + 1], None,
                                      ALU.mult).then_inc(xn_ready, 1)

            def gained_low(row, src, hi, lo, ready, before, signal):
                for d in range(DT):
                    if d % 2 == 0:
                        dve.wait_ge(ready, before + d + 2)
                    dve.scalar_tensor_tensor(lo[:, d, :], src(d),
                                             gains[:, row * DT + d:row * DT + d + 1], hi[:, d, :].bitcast(F32),
                                             ALU.mult, ALU.subtract).then_inc(signal, 1)

            def take_gathered(n):
                for half in range(2):
                    dve.wait_ge(xg_hi_ready, n + (half + 1))
                    s = slice(4 * half, 4 * half + 4)
                    mm = dve.tensor_tensor(xg_lo[:, s, :].rearrange("p d t -> p (d t)"), banks[GATHER[half]][:],
                                           xg_hi[:, s, :].bitcast(F32).rearrange("p d t -> p (d t)"), ALU.subtract)
                mm.then_inc(xg_lo_ready, 1)

            def take_output(n):
                for half in range(2):
                    dve.wait_ge(y_hi_ready, n + (half + 1))
                    s = slice(half * CW, (half + 1) * CW)
                    mm = dve.tensor_tensor(y_lo[:, s], banks[OUT[0][half]][:], y_hi[:, s].bitcast(F32), ALU.subtract)
                mm.then_inc(y_lo_ready, 1)

            def pick_tokens(ps, expert, before):
                for t in range(NT):
                    mm = dve.tensor_scalar(pick[:, t, :], consts[:, C_IOTA:C_IOTA + P],
                                           pos4[:, ps.block, t, expert], None, ALU.is_equal)
                mm.then_inc(picked, 1)

            def add_scattered(ps, expert, n):
                for t, pair in enumerate((OUT[0], GATHER)):
                    dve.wait_ge(scattered, n + (t + 1))
                    for half in range(2):
                        s = slice(half * CW, (half + 1) * CW)
                        mm = dve.scalar_tensor_tensor(x_res[:, t, s], banks[pair[half]][:], comb3[:, t, expert],
                                                      x_res[:, t, s], ALU.mult, ALU.add)
                    mm.then_inc(added, 1)

            def feed_forward(ps, e, ahead=0):
                for j, (kind, c, half) in enumerate(FFN_UNITS):
                    if ps.moe and j == 2:
                        take_output(e * 2 + 2 * ps.x0)
                    for cc in range(NC):
                        if AT[("w3", cc, 1)] + NHI == j:
                            dve.wait_ge(unit_used, ps.units(AT[("w3", cc, 1)] + 1, e))
                            dve.wait_ge(activated, ps.chunks(cc + 1, e))
                            for t in range(ps.tiles):
                                mm = dve.tensor_tensor(hidden[:, t, :], hidden[:, t, :], banks[UP3[t]][:], ALU.mult)
                            mm.then_inc(gated, 1)
                    if ps.moe and j == SCATTER_AT + NHI:
                        if ps.x0:
                            dve.wait_ge(added, e * 2 + 2 * ps.x0)
                        add_scattered(ps, bass.ds(e, 1), e * 2 + 2 * ps.x0)
                    for cc in range(NC):
                        if TURN[cc] + NHI == j:
                            dve.wait_ge(hidden_hi, ps.chunks(cc + 1, e))
                            for t in range(ps.tiles):
                                hi = hm_hi[:, cc % 2, :] if ps.moe else b_hi[:, cc % 2, t, :]
                                lo = hm_lo[:, cc % 2, :] if ps.moe else b_lo[:, cc % 2, t, :]
                                mm = dve.tensor_tensor(lo, turn_bank(ps, cc, t)[:],
                                                       hi.bitcast(F32), ALU.subtract)
                            mm.then_inc(hidden_lo, 1)
                    if ps.moe and j == PICK_AT:
                        dve.wait_ge(pick_turned, e + (ps.p0 + 1))
                        pick_tokens(ps, bass.ds(e + 1, 1), e)
                    if j >= ahead:
                        split(ps.u0 + j, ps, j, e)
                    if ps.moe and j == 0:
                        take_gathered(e * 2 + 2 * ps.p0)

            step(dve.memset(warm_in, 1.0))
            step(dve.memset(position[:], -1.0))
            step(dve.memset(combine[:], 0.0))
            for t in range(NT):
                dve.wait_ge(x_in[t], 16)
            normalise(0)
            dve.wait_ge(vec_turned, 1)
            step(dve.tensor_copy(gains[:], banks[7][:, 0:NV]))
            dve.wait_ge(consts_in, 16)
            dve.tensor_scalar(first_key, consts[:, C_IOTA:C_IOTA + E], -1.0, float(E), ALU.mult,
                              ALU.add).then_inc(gains_ready, 1)
            for b in range(4):
                dve.wait_ge(pooled, b + 1)
                for d in (2 * b, 2 * b + 1):
                    mm = dve.tensor_scalar(pooled_t[:, d, :], banks[b][:, (d % 2) * SEQ:(d % 2 + 1) * SEQ],
                                           gains[:, d:d + 1], None, ALU.mult)
                mm.then_inc(pooled_out, 1)
            for i in range(NHI):
                split(U_DENSE + i)
            dve.wait_ge(pool_ready, NT)
            for half in range(2):
                s = slice(half * CW, (half + 1) * CW)
                dve.wait_ge(mixed, half + 1)
                for t in range(NT):
                    y = pool_y[:, t * CW:(t + 1) * CW]
                    step(dve.tensor_tensor(y, banks[OUT[t][half]][:], pool_rows[:, 1, s], ALU.mult))
                    mm = dve.tensor_tensor(x_res[:, t, s], x_res[:, t, s], y, ALU.add)
                    if half:
                        mm.then_inc(x_ready, 1)
                    else:
                        step(mm)

            dve.wait_ge(x_ready, NT)
            normalise(1)
            gained_low(1, turned_x, a_hi, a_lo, a_hi_ready, 0, a_lo_ready)
            feed_forward(PASSES[0], 0, ahead=NHI)
            for i in range(NHI):
                if i == NHI - 1:
                    dve.wait_ge(unit_used, U_KV)
                    for t in range(NT):
                        for half in range(2):
                            s = slice(half * CW, (half + 1) * CW)
                            mm = dve.tensor_tensor(x_res[:, t, s], x_res[:, t, s], banks[OUT[t][half]][:], ALU.add)
                        mm.then_inc(x_ready, 1)
                split(U_KV + i)

            dve.wait_ge(x_ready, 2 * NT)
            normalise(2)
            gained_low(2, lambda d: xn_t[:, d, :], kv_hi, kv_lo, kv_hi_ready, 0, kv_lo_ready)
            gained_low(3, lambda d: xn_t[:, d, :], a_hi, a_lo, a_hi_ready, DT, a_lo_ready)
            sin = consts[:, C_SIN:C_SIN + SEQ]
            half_d = HD // 2
            for i, (n, b, _) in enumerate(ROPE):
                dve.wait_ge(biased, i + 1)
                for r in range(0, P, half_d):
                    to = r ^ half_d
                    mm = dve.tensor_tensor(rope_z[to:to + half_d, 0:n, :], rope_x[r:r + half_d, i % 2, 0:n, :],
                                           sin[r:r + half_d].unsqueeze(1).to_broadcast([half_d, n, SEQ]), ALU.mult)
                step(mm)
                dve.wait_ge(cosined, i + 1)
                if i:
                    def by_chunk(t_):
                        return t_.rearrange("p a (c t) -> p a c t", t=CHUNK)

                    dve.tensor_tensor(q_t[:, i - 1, :, :].rearrange("p c (a t) -> p a c t", a=2), by_chunk(rope_y[:]),
                                      by_chunk(rope_z[:]), ALU.add).then_inc(roped, 1)
                else:
                    for g in range(2):
                        for to in (0, HD):
                            s = slice(g * HD, (g + 1) * HD)
                            mm = dve.tensor_tensor(k_t[to:to + HD, g, :], rope_y[s, 0, :], rope_z[s, 0, :], ALU.add)
                    mm.then_inc(roped, 1)
                    dve.wait_ge(bv_in, 16)
                    dve.wait_ge(unit_used, U_KV + 1)
                    for to, c, of, t in ((0, 1, 0, 0), (64, 1, 64, 0), (0, 2, 64, 0), (64, 2, 0, 1), (0, 3, 0, 1),
                                         (64, 3, 64, 1), (0, 0, 0, 0), (64, 0, 0, 0)):
                        mm = dve.tensor_tensor(v_win[to:to + CHUNK, c, :], banks[5][of:of + CHUNK, t * P:(t + 1) * P],
                                               b_v[of:of + CHUNK, :], ALU.add)
                    mm.then_inc(v_out, 1)
                dve.wait_ge(roped, i + 1)
                split(U_KV + NHI + i)

            dve.wait_ge(misc_in, 16 * 2)
            for a in range(2):
                rows = slice(a * CHUNK, (a + 1) * CHUNK)
                mm = dve.tensor_copy(sinks[rows, :].rearrange("p (g r b) -> p g r b", g=2, r=2),
                                     sink_row[rows, :].rearrange("p (g b a r) -> p a g r b", g=2, a=2, b=2)[:, a])
            step(mm)
            step(dve.tensor_scalar(neg_sinks[:], sinks[:], -1.0, None, ALU.mult))

            def maxima_of(i):
                c, j0, n, nk = STEPS[i]
                dve.wait_ge(scored, i + 1)
                if i >= 2:
                    dve.wait_ge(exped, i - 1)
                step(dve.tensor_reduce(stat(maxima, i), banks[i % 2][:].rearrange("p (h k) -> p h k", h=n), AX_X,
                                       ALU.max))
                step(dve.scalar_tensor_tensor(stat(neg_max, i), stat(maxima, i), -(HD ** -0.5),
                                              neg_sinks[:, j0:j0 + n], ALU.mult, ALU.min))
                dve.tensor_tensor(stat(sink_in, i), sinks[:, j0:j0 + n], stat(neg_max, i), ALU.add).then_inc(max_ready, 1)

            def weigh(i):
                c, j0, n, nk = STEPS[i]
                dve.wait_ge(exped, i + 1)
                step(dve.tensor_tensor(denom[:, 0:n], stat(sums, i), stat(sink_exp, i), ALU.add))
                step(dve.reciprocal(stat(recip, i), denom[:, 0:n]))
                sc = probs[:, i % 2, :].rearrange("p (h k) -> p h k", h=n)
                dve.tensor_tensor(sc, sc, stat(recip, i).unsqueeze(2).to_broadcast([P, n, nk]),
                                  ALU.mult).then_inc(weighted, 1)

            for i in range(NS + 1):
                if i < NS:
                    maxima_of(i)
                if i >= 1:
                    weigh(i - 1)
            for b in range(4):
                dve.wait_ge(ot_hi_ready, b + 1)
                dve.tensor_tensor(ot_lo[:, 2 * b:2 * b + 2, :].rearrange("p d t -> p (d t)"), banks[4 + b][:],
                                  ot_hi[:, 2 * b:2 * b + 2, :].bitcast(F32).rearrange("p d t -> p (d t)"),
                                  ALU.subtract).then_inc(ot_lo_ready, 1)
            split(U_O + 3)
            dve.wait_ge(unit_used, U_O + 4)
            dve.wait_ge(bo_added, NT)
            for t in range(NT):
                for half in range(2):
                    s = slice(half * CW, (half + 1) * CW)
                    mm = dve.tensor_tensor(x_res[:, t, s], x_res[:, t, s], banks[PROJ[t][half]][:], ALU.add)
                mm.then_inc(x_ready, 1)

            dve.wait_ge(x_ready, 3 * NT)
            norm(3)
            dve.wait_ge(gn_in, 16)
            for t in range(NT):
                dve.scalar_tensor_tensor(xn[:, t, :], x_res[:, t, :], rstd[:, t:t + 1], row_bc[:],
                                         ALU.mult, ALU.mult).then_inc(gained, 1)
            dve.wait_ge(gained, NT)
            for t in range(NT):
                dve.wait_ge(xs_hi_ready, t + 1)
                dve.tensor_tensor(xs_lo[:, t, :], xn[:, t, :], xs_hi[:, t, :].bitcast(F32),
                                  ALU.subtract).then_inc(xs_lo_ready, 1)
            dve.wait_ge(routed, 1)
            step(dve.tensor_copy(logits[:], banks[4][:, 0:NT * E]))
            for t in range(NT):
                step(dve.max(top[:, t * 8:t * 8 + 8], logits[:, t * E:(t + 1) * E]))
            tops = view3(top, NT)
            dve.tensor_tensor(gate_w[:, 0:2], tops[:, :, 1], tops[:, :, 0], ALU.subtract).then_inc(gate_in, 1)
            def per_tile(column):
                return column.unsqueeze(2).to_broadcast([P, NT, E])

            keys = first_key.unsqueeze(1).to_broadcast([P, NT, E])
            eq3, run3 = view3(eq, NT), view3(run, NT)
            for rank, (of, to) in enumerate(((logits, first), (rest, second))):
                step(dve.tensor_tensor(eq3, view3(of, NT), per_tile(tops[:, :, rank]), ALU.is_equal))
                step(dve.tensor_tensor(run3, eq3, keys, ALU.mult))
                step(dve.tensor_reduce(best, run3, AX_X, ALU.max))
                step(dve.tensor_tensor(view3(to, NT), run3, per_tile(best), ALU.is_equal))
                if rank == 0:
                    step(dve.scalar_tensor_tensor(rest[:], first[:], -3e38, logits[:], ALU.mult, ALU.add))
            dve.tensor_tensor(chosen[:], first[:], second[:], ALU.add).then_inc(chosen_ready, 1)
            dve.wait_ge(counted, 1)
            step(dve.tensor_tensor(run[:], banks[5][:, 0:NT * E], chosen[:], ALU.mult))
            step(dve.tensor_scalar(pos4[:, 0, :, 0:E], run3, -1.0, None, ALU.add))

            def finish_routing():
                step(dve.tensor_scalar(pos4[:, 1, :, :], pos4[:, 0, :, :], -float(P), None, ALU.add))
                step(dve.tensor_reduce(over[:, 0:1], banks[5][:, 2 * E:3 * E], AX_X, ALU.max))
                dve.tensor_scalar(over_flag[:], over[:, 0:1], float(P), None, ALU.is_gt).then_inc(flag_ready, 1)
                dve.wait_ge(gate_exp, 1)
                step(dve.tensor_scalar(gate_w[:, 0:2], gate_w[:, 2:4], 1.0, None, ALU.add))
                step(dve.reciprocal(gate_w[:, 0:2], gate_w[:, 0:2]))
                step(dve.tensor_tensor(gate_w[:, 2:4], gate_w[:, 2:4], gate_w[:, 0:2], ALU.mult))
                step(dve.tensor_tensor(run3, view3(second, NT), per_tile(gate_w[:, 2:4]), ALU.mult))
                step(dve.tensor_tensor(eq3, view3(first, NT), per_tile(gate_w[:, 0:2]), ALU.mult))
                step(dve.tensor_tensor(comb3[:, :, 1:E + 1], eq3, run3, ALU.add))

            def expert_pass(ps):
                if ps.x0:
                    dve.wait_ge(pick_turned, ps.p0)
                    dve.wait_ge(gathered, ps.x0)
                pick_tokens(ps, slice(0, 1), 0)
                if not ps.x0:
                    finish_routing()
                with dve.Fori(0, E) as e:
                    feed_forward(ps, e)
                take_output(2 * (ps.x0 + E))
                dve.wait_ge(added, 2 * (ps.x0 + E))
                add_scattered(ps, slice(E, E + 1), 2 * (ps.x0 + E))
                dve.wait_ge(added, 2 * (ps.x0 + E + 1))

            expert_pass(PASSES[1])
            dve.wait_ge(flag_ready, 1)
            again = dve.value_load(over_flag[0:1, 0:1], min_val=0, max_val=1)
            with dve.If(again > 0):
                expert_pass(PASSES[2])

            dve.memset(var[:], 0.0).then_inc(stream_done, 1)
            norm(4)
            dve.wait_ge(gf_in, 16)
            for t in range(NT):
                dve.scalar_tensor_tensor(xn[:, t, :], x_res[:, t, :], rstd[:, t:t + 1], row_bc[:],
                                         ALU.mult, ALU.mult).then_inc(xn_ready, 1)


_INS = ["x", "norm_mix", "norm_ffn", "pool_w", "pool_b", "pool_scale", "norm_kv", "w_kv", "b_kv", "w_q", "b_q",
        "attn_sinks", "w_o", "b_o", "ffn_w1", "ffn_w3", "ffn_w2", "router_w", "moe_w1", "moe_w3", "moe_w2",
        "norm_final"]


def kernel(**inputs):
    import concourse.bacc as bacc
    from concourse.bass_utils import run_bass_kernel_spmd

    table, bands = shape_constants()
    nc = bacc.Bacc("TRN2", target_bir_lowering=False, num_devices=1)
    arrays = {f"in_{name}": np.ascontiguousarray(inputs[name]) for name in _INS}
    arrays["in_table"] = table
    arrays["in_bands"] = bands
    args = [nc.dram_tensor(name, a.shape, mybir.dt.from_np(a.dtype), kind="ExternalInput").ap()
            for name, a in arrays.items()]
    out = nc.dram_tensor("out_x", (1, SEQ, D), F32, kind="ExternalOutput").ap()
    trunk_program(nc, *args, out)
    result = run_bass_kernel_spmd(nc, [arrays], core_ids=[0])
    return result.results[0]["out_x"]
```

```python
import numpy as np
from contextlib import ExitStack

import concourse.bass as bass
from concourse import mybir

F32 = mybir.dt.float32
F32R = mybir.dt.float32r
I32 = mybir.dt.int32
ALU = mybir.AluOpType
ACT = mybir.ActivationFunctionType
AX_X = mybir.AxisListType.X

P = 128
SEQ = 256
D = 1024
F = 3584
E = 8
HD = 64
NH = 16
CHUNK = 64
WINDOWS = (2, 4, 8, 16)
NT = SEQ // P
NPAIR = NH // 2
DT = D // P
CW = 512
NC = F // CW
UNIT = 2048
RING = 14
NHI = 3
EPS = 1e-5

FFN_UNITS = []
for _c in range(NC + 1):
    if _c < NC:
        FFN_UNITS += [("w1", _c, 0), ("w1", _c, 1), ("w3", _c, 0), ("w3", _c, 1)]
    if _c > 0:
        FFN_UNITS += [("w2", _c - 1, 0), ("w2", _c - 1, 1)]
NU = len(FFN_UNITS)
AT = {key: j for j, key in enumerate(FFN_UNITS)}
TURN = {c: AT[("w2", c - 1, 0)] if c else AT[("w1", 1, 1)] for c in range(NC)}
SCATTER_AT = AT[("w3", 0, 1)]
GATHER_AT = AT[("w2", NC - 2, 1)]
PICK_AT = AT[("w3", 2, 0)]

U_BAND, U_POOLW = 0, 1
U_DENSE = 2
U_KV = U_DENSE + NU
U_Q = U_KV + 1
U_O = U_Q + 4
U_MOE = (U_O + 4, U_O + 4 + E * NU)
assert NU % RING == 0 and NU % NHI == 0

C_ID, C_TRI, C_ONE, C_IOTA = 0, P, 2 * P, 3 * P
C_COS, C_SIN = 4 * P, 6 * P
C_N = 8 * P


def shape_constants():
    t = np.arange(SEQ)
    table = np.zeros((P, C_N), np.float32)
    table[:, C_ID:C_ID + P] = np.eye(P)
    table[:, C_TRI:C_TRI + P] = np.triu(np.ones((P, P)))
    table[:, C_ONE:C_ONE + P] = 1.0
    table[:, C_IOTA:C_IOTA + P] = np.arange(P)[None, :]
    half = HD // 2
    inv = (np.float32(10000.0) ** (-np.arange(half, dtype=np.float32) / half)).astype(np.float32)
    ang = t.astype(np.float32)[None, :] * inv[:, None]
    row = np.arange(P) % half
    table[:, C_COS:C_COS + SEQ] = np.cos(ang)[row]
    sign = np.where(np.arange(P) % HD < half, 1.0, -1.0)[:, None]
    table[:, C_SIN:C_SIN + SEQ] = np.sin(ang)[row] * sign
    bands = np.zeros((len(WINDOWS), SEQ, SEQ), np.float32)
    for g, win in enumerate(WINDOWS):
        back = t[None, :] - t[:, None]
        mean = ((back >= 0) & (back < win)) / np.minimum(t + 1, win)[None, :].astype(np.float32)
        bands[g] = mean.astype(np.float32) - np.eye(SEQ, dtype=np.float32)
    bands = bands.reshape(len(WINDOWS), NT, P, SEQ).transpose(2, 0, 1, 3)
    return table, np.ascontiguousarray(bands.reshape(P, -1))


def trunk_program(nc, x, norm_mix, norm_ffn, pool_w, pool_b, pool_scale, norm_kv, w_kv, b_kv, w_q, b_q,
                  attn_sinks, w_o, b_o, ffn_w1, ffn_w3, ffn_w2, router_w, moe_w1, moe_w3, moe_w2,
                  norm_final, table, bands, out):
    ctx = ExitStack()
    with ctx:
        K = 1024
        arena_bytes = (RING + NHI) * UNIT * 4 + 64 * K + P * 4 + C_N * 4 + 2 * K
        arena = ctx.enter_context(nc.sbuf_tensor("arena", [P, arena_bytes // 4], F32))
        base = nc.sbuf_base - arena_bytes
        end = [base]

        def at(name, shape, dtype, offset):
            return nc.alloc_sbuf_tensor_at(name, shape, dtype, offset=offset)

        def place(nbytes):
            end[0] += nbytes
            assert end[0] <= base + arena_bytes
            return end[0] - nbytes

        o_raw = place(RING * UNIT * 4)
        raw = [at(f"raw{r}", [P, UNIT], F32, o_raw + r * UNIT * 4) for r in range(RING)]
        low = [at(f"low{r}", [P, UNIT], F32R, o_raw + r * UNIT * 4) for r in range(RING)]
        high = [at(f"high{r}", [P, UNIT], F32R, place(UNIT * 4)) for r in range(NHI)]
        x_res = at("x_res", [P, NT, D], F32, place(8 * K))
        o_a = place(16 * K)
        o_b = place(16 * K)
        o_w = place(20 * K)
        row_bc = at("row_bc", [P, D], F32, place(4 * K))
        consts = at("consts", [P, C_N], F32, place(C_N * 4))
        b_v = at("b_v", [P, P], F32, place(P * 4))
        o_s = place(2 * K)

        a_hi = at("a_hi", [P, DT, SEQ], F32R, o_a)
        a_lo = at("a_lo", [P, DT, SEQ], F32R, o_a + 8 * K)
        xg_hi = at("xg_hi", [P, DT, P], F32R, o_a)
        xg_lo = at("xg_lo", [P, DT, P], F32R, o_a + 8 * K)
        ot_hi, ot_lo = a_hi, a_lo
        squares = at("squares", [P, NT, D], F32, o_a)
        b_hi = at("b_hi", [P, 2, NT, CW], F32R, o_b)
        b_lo = at("b_lo", [P, 2, NT, CW], F32R, o_b + 8 * K)
        pool_rows = at("pool_rows", [P, 2, D], F32, o_b)
        pool_bs = at("pool_bs", [P, D], F32, o_b + 8 * K)
        kv_hi = b_hi[:].rearrange("p a b c -> p (a b c)").rearrange("p (d t) -> p d t", d=DT)
        kv_lo = b_lo[:].rearrange("p a b c -> p (a b c)").rearrange("p (d t) -> p d t", d=DT)
        probs = at("probs", [P, 2, CW], F32, o_b)
        probs_t = at("probs_t", [P, 2, CW], F32, o_b + 4 * K)
        xs_hi = b_hi[:].rearrange("p a b c -> p (a b c)").rearrange("p (t d) -> p t d", t=NT)
        xs_lo = b_lo[:].rearrange("p a b c -> p (a b c)").rearrange("p (t d) -> p t d", t=NT)
        pooled_t = at("pooled_t", [P, DT, SEQ], F32, o_w)
        q_t = at("q_t", [P, NH // 4, SEQ // CHUNK, 2 * CHUNK], F32, o_w)
        h_t = at("h_t", [P, DT, SEQ], F32, o_w)
        xn = at("xn", [P, NT, D], F32, o_w + 8 * K)
        rope_x = at("rope_x", [P, 2, 2, SEQ], F32, o_w + 8 * K)
        rope_y = at("rope_y", [P, 2, SEQ], F32, o_w + 12 * K)
        rope_z = at("rope_z", [P, 2, SEQ], F32, o_w + 14 * K)
        hidden = at("hidden", [P, NT, CW], F32, o_w + 16 * K)
        k_t = at("k_t", [P, 2, SEQ], F32, o_w + 16 * K)
        v_win = at("v_win", [P, SEQ // CHUNK, P], F32, o_w + 18 * K)
        hm_hi = at("hm_hi", [P, 2, CW], F32R, o_w)
        hm_lo = at("hm_lo", [P, 2, CW], F32R, o_w + 4 * K)
        y_hi = at("y_hi", [P, D], F32R, o_w + 8 * K)
        y_lo = at("y_lo", [P, D], F32R, o_w + 12 * K)
        pick = at("pick", [P, NT, P], F32R, o_w + 18 * K)
        pick_t = at("pick_t", [P, SEQ], F32R, o_w + 19 * K)
        smalls = at("smalls", [P, 512], F32, o_s)
        small_at = [0]

        def small(n):
            small_at[0] += n
            assert small_at[0] <= 512
            return smalls[:, small_at[0] - n:small_at[0]]

        NV = 5 * DT + 1
        gains = small(NV)
        sinks = small(NPAIR)
        neg_sinks = small(NPAIR)
        sink_row = small(NH)
        sumsq = small(NT)
        var = small(NT)
        std = small(NT)
        rstd = small(NT)
        maxima = small(2 * NPAIR)
        neg_max = small(2 * NPAIR)
        sums = small(2 * NPAIR)
        sink_in = small(2 * NPAIR)
        sink_exp = small(2 * NPAIR)
        denom = small(NPAIR)
        recip = small(2 * NPAIR)
        r_w = small(DT * E)
        logits = small(NT * E)
        top = small(NT * 8)
        eq = small(NT * E)
        run = small(NT * E)
        first = small(NT * E)
        second = small(NT * E)
        rest = small(NT * E)
        chosen = small(NT * E)
        gate_w = small(NT * 4)
        position = small(2 * NT * (E + 1))
        combine = small(2 * NT * (E + 1))
        first_key = small(E)
        warm_in = small(1)
        warm_out = small(1)
        best = small(NT)
        over = small(2)
        over_flag = small(1).bitcast(I32)
        vec_rows = at("vec_rows", [NV, P], F32, o_a)

        banks = [ctx.enter_context(nc.psum_tensor(f"bank{i}", [P, CW], F32)) for i in range(8)]
        UP1, UP3 = (0, 1), (2, 3)
        OUT = ((4, 5), (6, 7))
        TURN_BANK, PICK_BANK, GATHER = 1, 3, (6, 7)
        LOGITS = (0, 1)
        PROJ = ((0, 1), (2, 3))

        def view3(t, n):
            return t[:].rearrange("p (a b) -> p a b", a=n)

        ident = consts[:, C_ID:C_ID + P]
        pos4 = position[:].rearrange("p (s t e) -> p s t e", s=2, t=NT)
        comb4 = combine[:].rearrange("p (s t e) -> p s t e", s=2, t=NT)

        def sem(name):
            return ctx.enter_context(nc.semaphore(name))

        landed = [sem(f"landed{r}") for r in range(RING)]
        split_hi, split_lo = sem("split_hi"), sem("split_lo")
        unit_used = sem("unit_used")
        x_in = [sem(f"x_in{t}") for t in range(NT)]
        consts_in, vec_in, pool_in = sem("consts_in"), sem("vec_in"), sem("pool_in")
        misc_in, bo_in, bv_in = sem("misc_in"), sem("bo_in"), sem("bv_in")
        gn_in, gf_in, out_done = sem("gn_in"), sem("gf_in"), sem("out_done")
        sumsq_ready, var_ready, std_ready = sem("sumsq_ready"), sem("var_ready"), sem("std_ready")
        xn_ready = sem("xn_ready")
        x_ready = sem("x_ready")
        stream_done = sem("stream_done")
        vec_turned, gains_ready = sem("vec_turned"), sem("gains_ready")
        pool_scaled, pool_ready = sem("pool_scaled"), sem("pool_ready")
        pooled, pooled_out, mixed = sem("pooled"), sem("pooled_out"), sem("mixed")
        turned, a_hi_ready, a_lo_ready = sem("turned"), sem("a_hi_ready"), sem("a_lo_ready")
        dense_out, proj_out = sem("dense_out"), sem("proj_out")
        activated, gated, hidden_turned = sem("activated"), sem("gated"), sem("hidden_turned")
        hidden_hi, hidden_lo = sem("hidden_hi"), sem("hidden_lo")
        kv_hi_ready, kv_lo_ready, kv_done, v_out = sem("kv_hi_ready"), sem("kv_lo_ready"), sem("kv_done"), sem("v_out")
        biased, cosined, roped = sem("biased"), sem("cosined"), sem("roped")
        scored, half_scored, max_ready, exped = sem("scored"), sem("half_scored"), sem("max_ready"), sem("exped")
        weighted, probs_turned = sem("weighted"), sem("probs_turned")
        probs_out, attended = sem("probs_out"), sem("attended")
        ot_hi_ready, ot_lo_ready, bo_added = sem("ot_hi_ready"), sem("ot_lo_ready"), sem("bo_added")
        gained, xs_hi_ready, xs_lo_ready = sem("gained"), sem("xs_hi_ready"), sem("xs_lo_ready")
        h_out, routed, gate_in, gate_exp = sem("h_out"), sem("routed"), sem("gate_in"), sem("gate_exp")
        chosen_ready, counted, flag_ready = sem("chosen_ready"), sem("counted"), sem("flag_ready")
        picked, gathered = sem("picked"), sem("gathered")
        xg_hi_ready, xg_lo_ready = sem("xg_hi_ready"), sem("xg_lo_ready")
        pick_turned, pick_t_ready = sem("pick_turned"), sem("pick_t_ready")
        y_hi_ready, y_lo_ready = sem("y_hi_ready"), sem("y_lo_ready")
        scattered, added = sem("scattered"), sem("added")
        last_hi, last_lo, last_scattered = sem("last_hi"), sem("last_lo"), sem("last_scattered")
        dve_step, pool_step = sem("dve_step"), sem("pool_step")

        x_d = x.rearrange("o (t p) d -> p (o t) d", p=P)
        out_d = out.rearrange("o (t p) d -> p (o t) d", p=P)

        def up_view(w):
            return w.rearrange("o (k p) f -> o p k f", p=P)

        dense = {"w1": up_view(ffn_w1), "w3": up_view(ffn_w3), "w2": up_view(ffn_w2)}
        experts = {n: w.rearrange("o e (k p) f -> (o e) p k f", p=P)
                   for n, w in (("w1", moe_w1), ("w3", moe_w3), ("w2", moe_w2))}

        def bc(row):
            return row.rearrange("(o n) -> o n", o=1).to_broadcast([P, row.shape[0]])

        def ffn_source(views, e, kind, c, half):
            if kind == "w2":
                part = views[kind][bass.ds(e, 1), :, 4 * c + 2 * half:4 * c + 2 * half + 2, :]
            else:
                part = views[kind][bass.ds(e, 1), :, 4 * half:4 * half + 4, c * CW:(c + 1) * CW]
            return part.rearrange("o p k f -> p (o k) f")

        def slot(u):
            return u % RING

        def turn_bank(ps, c, t):
            return banks[TURN_BANK if ps.moe else OUT[0][t] if c == 0 else UP1[t]]

        def hslot(u):
            return (u - U_DENSE) % NHI

        def turned_x(d):
            return banks[2 + d // 2][:, (d % 2) * SEQ:(d % 2 + 1) * SEQ]

        def kv_x(d):
            return banks[d // 2][:, (d % 2) * SEQ:(d % 2 + 1) * SEQ]

        def raw3(u, k):
            return raw[slot(u)][:].rearrange("p (k f) -> p k f", k=k)

        def hi3(u, k):
            return high[hslot(u)][:].rearrange("p (k f) -> p k f", k=k)

        def lo3(u, k):
            return low[slot(u)][:].rearrange("p (k f) -> p k f", k=k)

        class Pass:

            def __init__(self, n):
                self.moe = n > 0
                self.tiles = 1 if n else NT
                self.block = n - 1
                self.u0 = U_MOE[n - 1] if n else U_DENSE
                self.k0 = NC + (n - 1) * E * NC if n else 0
                self.p0 = (n - 1) * E
                self.lists = (n - 1) * (E + 1)

            def units(self, j, e):
                return e * NU + (self.u0 + j) if self.moe else self.u0 + j

            def chunks(self, c, e):
                return e * NC + (self.k0 + c) if self.moe else self.k0 + c

        PASSES = [Pass(0), Pass(1), Pass(2)]

        STEPS = ([(c, 0, 4, 2 * CHUNK) for c in (1, 2, 3)] + [(0, 0, NPAIR, CHUNK)]
                 + [(c, 4, 4, 2 * CHUNK) for c in (1, 2, 3)])
        NS = len(STEPS)
        O_SPLITS = {3: 1, 5: 2}

        def pair(j):
            return j // 4 * 2 + j % 2, j // 2 % 2

        def stat(t_, i):
            return t_[:, NPAIR * (i % 2):NPAIR * (i % 2) + STEPS[i][2]]

        ROPE = [(1, 4, 5 * DT)] + [(2, 6 + m % 2, 4 * DT + 2 * m) for m in range(4)]

        def vector_loads(engine, first, last):
            vectors = (norm_mix[0], norm_ffn[0], norm_kv, norm_mix[1], b_q[0], b_kv[0:P])
            for i in range(first, last):
                v = vectors[i]
                engine.dma_start(vec_rows[i * DT:i * DT + v.shape[0] // P, :],
                                 v.rearrange("(d p) -> d p", p=P)).then_inc(vec_in, 16)

        block = ctx.enter_context(nc.Block())

        @block.sync
        def _(sp):
            def load(u, src, k, used=None):
                used = u - RING + 1 if used is None else used
                if not isinstance(used, int) or used > 0:
                    sp.wait_ge(unit_used, used)
                sp.dma_start(raw3(u, k), src).then_inc(landed[slot(u)], 16)

            for t in range(NT):
                sp.dma_start(x_res[:, t, :], x_d[:, t, :]).then_inc(x_in[t], 16)
            vector_loads(sp, 0, 4)
            sp.dma_start(pool_rows[:, 1, :], bc(pool_scale[0])).then_inc(pool_in, 16)
            load(U_BAND, bands.rearrange("p (k f) -> p k f", k=8), 8)
            load(U_POOLW, pool_w.rearrange("o g (k p) f -> p (o g k) f", p=P), 8)
            sp.dma_start(pool_rows[:, 0, :], bc(pool_b.rearrange("o g d -> (o g d)"))).then_inc(pool_in, 16)
            for j, key in enumerate(FFN_UNITS):
                load(U_DENSE + j, ffn_source(dense, 0, *key), 2 if key[0] == "w2" else 4)
            load(U_KV, w_kv.rearrange("(k p) f -> p k f", p=P), DT)
            for m in range(4):
                load(U_Q + m, w_q[0].rearrange("(k p) f -> p k f", p=P)[:, :, m * SEQ:(m + 1) * SEQ], DT)
            for m in range(4):
                load(U_O + m, w_o[0].rearrange("(k p) f -> p k f", p=P)[:, 2 * m:2 * m + 2, :], 2)

            def expert_loads(ps):
                with sp.Fori(0, E) as e:
                    for j, key in enumerate(FFN_UNITS):
                        load(ps.u0 + j, ffn_source(experts, e, *key), 2 if key[0] == "w2" else 4,
                             ps.units(j - RING + 1, e))

            expert_loads(PASSES[1])
            sp.wait_ge(flag_ready, 1)
            again = sp.value_load(over_flag[0:1, 0:1], min_val=0, max_val=1)
            with sp.If(again > 0):
                expert_loads(PASSES[2])
            for t in range(NT):
                sp.wait_ge(xn_ready, 3 * NT + t + 1)
                sp.dma_start(out_d[:, t, :], xn[:, t, :]).then_inc(out_done, 16)
            sp.wait_ge(out_done, 16 * NT)

        @block.gpsimd
        def _(pool):
            pool.wait_ge(pool_in, 32)
            pool.tensor_tensor(pool_bs[:], pool_rows[:, 0, :], pool_rows[:, 1, :], ALU.mult).then_inc(pool_step, 1)
            pool.wait_ge(pool_step, 1)
            pool.wait_ge(xn_ready, NT)
            for t in range(NT):
                pool.tensor_tensor(x_res[:, t, :], x_res[:, t, :], pool_bs[:], ALU.add).then_inc(pool_ready, 1)
            pool.wait_ge(xn_ready, 3 * NT)
            pool.dma_start(b_v[:], bc(b_kv[P:2 * P])).then_inc(bv_in, 16)
            pool.wait_ge(bo_in, 16)
            for t in range(NT):
                pool.tensor_tensor(x_res[:, t, :], x_res[:, t, :], row_bc[:], ALU.add).then_inc(bo_added, 1)
            for i, (n, _, _) in enumerate(ROPE):
                pool.wait_ge(biased, i + 1)
                if i:
                    pool.wait_ge(roped, i)
                pool.tensor_tensor(rope_y[:, 0:n, :], rope_x[:, i % 2, 0:n, :],
                                   consts[:, C_COS:C_COS + SEQ].unsqueeze(1).to_broadcast([P, n, SEQ]),
                                   ALU.mult).then_inc(cosined, 1)
            pool.wait_ge(bo_added, NT)
            pool.dma_start(row_bc[:], bc(norm_ffn[1])).then_inc(gn_in, 16)
            pool.wait_ge(gained, NT)
            pool.dma_start(row_bc[:], bc(norm_final)).then_inc(gf_in, 16)
            pool.memset(pick_t[:].bitcast(F32), 0.0).then_inc(pick_t_ready, 1)

        @block.tensor
        def _(pe):
            def three_passes(o, s_hi, s_lo, m_hi, m_lo, start, stop):
                pe.matmul(o, s_hi, m_hi, start=start, stop=False)
                pe.matmul(o, s_lo, m_hi, start=False, stop=False)
                return pe.matmul(o, s_hi, m_lo, start=False, stop=stop)

            def keep_warm(bank, n):
                for _ in range(n):
                    pe.matmul(banks[bank][:, 0:P], ident, ident, start=True, stop=True)

            def turn_stream(ready, before, bank=0):
                for t in range(NT):
                    pe.wait_ge(ready, before + t + 1)
                    for d in range(DT):
                        at_ = (d % 2) * SEQ + t * P
                        mm = pe.transpose(banks[bank + d // 2][:, at_:at_ + P], xn[:, t, d * P:(d + 1) * P], ident)
                        if t == NT - 1 and d % 2:
                            mm.then_inc(turned, 1)

            def gather():
                for d in range(DT):
                    o = banks[GATHER[d // 4]][:, (d % 4) * P:(d % 4 + 1) * P]
                    for t in range(NT):
                        pe.matmul(o, xs_hi[:, t, d * P:(d + 1) * P], pick[:, t, :], start=t == 0, stop=False)
                        mm = pe.matmul(o, xs_lo[:, t, d * P:(d + 1) * P], pick[:, t, :],
                                       start=False, stop=t == NT - 1)
                mm.then_inc(gathered, 1)

            def scatter(signal):
                for t, pair in enumerate((OUT[0], GATHER)):
                    s = pick_t[:, t * P:(t + 1) * P]
                    for half in range(2):
                        m = slice(half * CW, (half + 1) * CW)
                        pe.matmul(banks[pair[half]][:], s, y_hi[:, m], start=True, stop=False)
                        mm = pe.matmul(banks[pair[half]][:], s, y_lo[:, m], start=False, stop=True)
                    mm.then_inc(signal, 1)

            def feed_forward(ps, e):
                act_hi, act_lo = (xg_hi, xg_lo) if ps.moe else (a_hi, a_lo)
                for j, (kind, c, half) in enumerate(FFN_UNITS):
                    u = ps.u0 + j
                    pe.wait_ge(split_lo, ps.units(j - U_DENSE + 1, e))
                    if half == 0 and kind == "w1":
                        if ps.moe or c == 1:
                            pe.wait_ge(activated, ps.chunks(c, e))
                        elif c:
                            pe.wait_ge(hidden_lo, ps.chunks(c, e))
                        if c == 0 and ps.moe:
                            pe.wait_ge(xg_lo_ready, e + (ps.p0 + 1))
                    if half == 0 and kind == "w3" and (ps.moe or c):
                        pe.wait_ge(gated, ps.chunks(c, e))
                    if kind == "w2" and half == 0:
                        pe.wait_ge(hidden_lo, ps.chunks(c + 1, e))
                        if c == 0 and ps.moe:
                            pe.wait_ge(added, e * 2 + (2 * ps.p0 + 1))
                    if kind == "w2":
                        for t in range(ps.tiles):
                            for ft in range(2):
                                i = 2 * half + ft
                                s = slice(i * P, (i + 1) * P)
                                s_hi = hm_hi[:, c % 2, s] if ps.moe else b_hi[:, c % 2, t, s]
                                s_lo = hm_lo[:, c % 2, s] if ps.moe else b_lo[:, c % 2, t, s]
                                for nh in range(2):
                                    m = slice(nh * CW, (nh + 1) * CW)
                                    mm = three_passes(banks[OUT[t][nh]][:], s_hi, s_lo,
                                                      hi3(u, 2)[:, ft, m], lo3(u, 2)[:, ft, m],
                                                      c == 0 and i == 0, c == NC - 1 and i == 3)
                            if j == NU - 1 and not ps.moe and t < NT - 1:
                                mm.then_inc(dense_out, 1)
                    else:
                        up = UP1 if kind == "w1" else UP3
                        for k in range(4):
                            d = 4 * half + k
                            if kind == "w1" and c == 0 and not ps.moe:
                                pe.wait_ge(a_lo_ready, d + 1)
                            for t in range(ps.tiles):
                                s = slice(t * P, (t + 1) * P)
                                mm = three_passes(banks[up[t]][:], act_hi[:, d, s], act_lo[:, d, s],
                                                  hi3(u, 4)[:, k, :], lo3(u, 4)[:, k, :], d == 0, d == DT - 1)
                    mm.then_inc(unit_used, 1)
                    if ps.moe and j == SCATTER_AT:
                        pe.wait_ge(y_lo_ready, e + (ps.p0 + 1))
                        pe.wait_ge(pick_t_ready, e + (ps.p0 + 1))
                        scatter(scattered)
                        for t in range(NT):
                            mm = pe.transpose(banks[PICK_BANK][:, t * P:(t + 1) * P],
                                              pick[:, t, :].bitcast(F32), ident)
                        mm.then_inc(pick_turned, 1)
                    for cc in range(NC):
                        if TURN[cc] == j:
                            pe.wait_ge(gated, ps.chunks(cc + 1, e))
                            for t in range(ps.tiles):
                                for i in range(4):
                                    mm = pe.transpose(turn_bank(ps, cc, t)[:, i * P:(i + 1) * P],
                                                      hidden[:, t, i * P:(i + 1) * P], ident)
                            mm.then_inc(hidden_turned, 1)
                    if ps.moe and j == GATHER_AT:
                        with pe.If(e < E - 1):
                            pe.wait_ge(picked, e + (ps.lists + 2))
                            pe.wait_ge(added, e * 2 + (2 * ps.p0 + 2))
                            gather()

            pe.wait_ge(consts_in, 16)
            keep_warm(0, 12)
            pe.wait_ge(xn_ready, NT)
            pe.wait_ge(landed[U_BAND], 16)
            band = raw3(U_BAND, 8)
            reach = max(WINDOWS)
            for d in range(DT):
                o, s, g = banks[d // 2], slice(d * P, (d + 1) * P), d // 2
                at_ = (d % 2) * SEQ
                pe.matmul(o[:, at_ + P:at_ + SEQ], xn[:, 1, s], band[:, g * NT + 1, P:SEQ], start=True, stop=False)
                pe.matmul(o[:, at_ + P:at_ + P + reach], xn[:, 0, s], band[:, g * NT, P:P + reach],
                          start=False, stop=False)
                mm = pe.matmul(o[:, at_:at_ + P], xn[:, 0, s], band[:, g * NT, 0:P], start=False, stop=True)
                if d % 2:
                    mm.then_inc(pooled, 1)
                if d == 0:
                    pe.wait_ge(vec_in, 16 * 6)
                    pe.transpose(banks[7][:, 0:NV], vec_rows[:, :], ident[0:NV, 0:NV]).then_inc(vec_turned, 1)
            pe.wait_ge(pooled, DT // 2)
            pe.wait_ge(landed[U_POOLW], 16)
            pe.wait_ge(gains_ready, 1)
            w = raw3(U_POOLW, 8)
            for t in range(NT):
                for g in range(len(WINDOWS)):
                    if t == 0:
                        pe.wait_ge(pool_scaled, g // 2 + 1)
                        pe.wait_ge(pooled_out, g + 1)
                    for k in range(2):
                        mm = pe.matmul(banks[OUT[t][g // 2]][:, (g % 2) * SEQ:(g % 2 + 1) * SEQ],
                                       pooled_t[:, 2 * g + k, t * P:(t + 1) * P], w[:, 2 * g + k, :],
                                       start=k == 0, stop=k == 1)
                mm.then_inc(mixed, 1)
            pe.wait_ge(mixed, NT)
            pe.nop().then_inc(unit_used, 2)

            keep_warm(0, 20)
            turn_stream(xn_ready, NT, bank=2)
            feed_forward(PASSES[0], 0)

            keep_warm(0, 30)
            turn_stream(xn_ready, 2 * NT, bank=0)
            pe.wait_ge(split_lo, U_KV - U_DENSE + 1)
            wh, wl = hi3(U_KV, DT), lo3(U_KV, DT)
            for d in range(DT):
                pe.wait_ge(kv_lo_ready, d + 1)
                mm = three_passes(banks[4][:, 0:SEQ], wh[:, d, 0:P], wl[:, d, 0:P], kv_hi[:, d, :], kv_lo[:, d, :],
                                  d == 0, d == DT - 1)
            mm.then_inc(kv_done, 1)
            for t in range(NT):
                s = slice(t * P, (t + 1) * P)
                for d in range(DT):
                    mm = three_passes(banks[5][:, s], kv_hi[:, d, s], kv_lo[:, d, s], wh[:, d, P:2 * P],
                                      wl[:, d, P:2 * P], d == 0, d == DT - 1)
            mm.then_inc(unit_used, 1)
            def scores(i):
                c, j0, n, nk = STEPS[i]
                k0 = max(c - 1, 0) * CHUNK
                if i >= 2:
                    pe.wait_ge(exped, i - 1)
                for k, a in enumerate(sorted(range(n), key=lambda a: pair(j0 + a)[1])):
                    b, r = pair(j0 + a)
                    if k == n // 2:
                        mm.then_inc(half_scored, 1)
                        pe.wait_ge(half_scored, i + 1)
                    rows = slice(HD * r, HD * r + HD)
                    mm = pe.matmul(banks[i % 2][:, a * nk:(a + 1) * nk],
                                   q_t[rows, b, c, :],
                                   k_t[rows, b // 2, k0:k0 + nk], start=True, stop=True)
                mm.then_inc(scored, 1)

            def turn_probs(i):
                pe.wait_ge(weighted, i + 1)
                if i >= 2:
                    pe.wait_ge(probs_out, i - 1)
                for a in range(4):
                    mm = pe.transpose(banks[2 + i % 2][:, a * P:(a + 1) * P], probs[:, i % 2, a * P:(a + 1) * P], ident)
                mm.then_inc(probs_turned, 1)

            def attend(i):
                c, j0, n, nk = STEPS[i]
                pe.wait_ge(probs_out, i + 1)
                for a in range(n):
                    b, r = pair(j0 + a)
                    keys = slice(a % 2 * CHUNK, (a % 2 + 1) * CHUNK) if c == 0 else slice(0, P)
                    at_ = (a // 2 if c == 0 else a) * P
                    o = banks[4 + b][HD * r:HD * r + HD, :].rearrange("p (a t) -> p a t", a=2)
                    mm = pe.matmul(o[:, :, c * CHUNK:(c + 1) * CHUNK], v_win[keys, c, b // 2 * HD:(b // 2 + 1) * HD],
                                   probs_t[keys, i % 2, at_:at_ + P].rearrange("p (a t) -> p a t", a=2),
                                   start=True, stop=True)
                mm.then_inc(attended, 1)

            pe.wait_ge(a_lo_ready, 2 * DT)
            for m in range(4):
                u = U_Q + m
                pe.wait_ge(split_lo, u - U_DENSE + 1)
                if m == 3:
                    pe.wait_ge(roped, 3)
                    scores(0)
                    scores(1)
                if m >= 2:
                    pe.wait_ge(biased, m)
                for n in range(2):
                    for d in range(DT):
                        s = slice(n * P, (n + 1) * P)
                        mm = three_passes(banks[6 + m % 2][:, n * SEQ:(n + 1) * SEQ], hi3(u, DT)[:, d, s],
                                          lo3(u, DT)[:, d, s], a_hi[:, d, :], a_lo[:, d, :], d == 0, d == DT - 1)
                mm.then_inc(unit_used, 1)

            pe.wait_ge(v_out, 1)
            for i in range(1, NS + 2):
                if i + 1 == 3:
                    pe.wait_ge(roped, len(ROPE))
                if i + 1 < NS:
                    scores(i + 1)
                if i <= NS:
                    turn_probs(i - 1)
                if i >= 2:
                    attend(i - 2)
            keep_warm(0, 5)

            for m in range(4):
                u = U_O + m
                pe.wait_ge(ot_lo_ready, m + 1)
                pe.wait_ge(split_lo, u - U_DENSE + 1)
                for t in range(NT):
                    s = slice(t * P, (t + 1) * P)
                    for k in range(2):
                        d = 2 * m + k
                        for nh in range(2):
                            c = slice(nh * CW, (nh + 1) * CW)
                            mm = three_passes(banks[PROJ[t][nh]][:], ot_hi[:, d, s], ot_lo[:, d, s],
                                              hi3(u, 2)[:, k, c], lo3(u, 2)[:, k, c], d == 0, d == DT - 1)
                    if m == 3 and t < NT - 1:
                        mm.then_inc(proj_out, 1)
                mm.then_inc(unit_used, 1)

            keep_warm(7, 26)
            turn_stream(gained, 0, bank=4)
            keep_warm(2, 2)
            pe.wait_ge(misc_in, 16 * 2)
            for d in range(DT):
                if d % 2 == 0:
                    pe.wait_ge(h_out, d // 2 + 1)
                for t in range(NT):
                    mm = pe.matmul(banks[LOGITS[t]][:, 0:E], h_t[:, d, t * P:(t + 1) * P],
                                   r_w[:, d * E:(d + 1) * E], start=d == 0, stop=d == DT - 1)
            mm.then_inc(routed, 1)
            keep_warm(7, 6)
            pe.wait_ge(chosen_ready, 1)
            tri, ones = consts[:, C_TRI:C_TRI + P], consts[:, C_ONE:C_ONE + P]
            c0, c1 = chosen[:, 0:E], chosen[:, E:2 * E]
            pe.matmul(banks[5][:, 0:E], tri, c0, start=True, stop=True)
            pe.matmul(banks[5][:, E:2 * E], tri, c1, start=True, stop=False)
            pe.matmul(banks[5][:, E:2 * E], ones, c0, start=False, stop=True)
            pe.matmul(banks[5][:, 2 * E:3 * E], ones, c0, start=True, stop=False)
            pe.matmul(banks[5][:, 2 * E:3 * E], ones, c1, start=False, stop=True).then_inc(counted, 1)

            def expert_pass(ps):
                if not ps.p0:
                    keep_warm(7, 5)
                pe.wait_ge(picked, ps.lists + 1)
                pe.wait_ge(xs_lo_ready, NT)
                if ps.p0:
                    pe.wait_ge(added, 2 * ps.p0)
                gather()
                if not ps.p0:
                    keep_warm(0, 9)
                with pe.Fori(0, E) as e:
                    feed_forward(ps, e)
                pe.wait_ge(pick_t_ready, ps.p0 + E + 1)

            expert_pass(PASSES[1])
            pe.wait_ge(flag_ready, 1)
            again = pe.value_load(over_flag[0:1, 0:1], min_val=0, max_val=1)
            with pe.If(again > 0):
                expert_pass(PASSES[2])
            keep_warm(0, 14)
            pe.wait_ge(last_lo, 1)
            scatter(last_scattered)

        @block.scalar
        def _(act):
            def split(u, ps=None, j=0, e=0):
                r = slot(u)
                if ps is not None and ps.moe:
                    act.wait_ge(landed[r], e * (16 * NU // RING) + 16 * (u // RING + 1))
                    act.wait_ge(unit_used, ps.units(j - NHI + 1, e))
                else:
                    act.wait_ge(landed[r], 16 * (u // RING + 1))
                    if u - NHI >= U_DENSE:
                        act.wait_ge(unit_used, u - NHI + 1)
                act.activation(high[hslot(u)][:], raw[r][:], ACT.Copy).then_inc(split_hi, 1)

            def warm(func):
                act.activation(warm_out, warm_in, func)

            def norm(n, ready, dump=xn):
                if n:
                    warm(ACT.Sqrt)
                for t in range(NT):
                    act.wait_ge(*ready(t))
                    act.activation(dump[:, t, :], x_res[:, t, :], ACT.Square,
                                   accum_out=sumsq[:, t:t + 1]).then_inc(sumsq_ready, 1)
                    act.wait_ge(var_ready, NT * n + t + 1)
                    act.activation(std[:, t:t + 1], var[:, t:t + 1], ACT.Sqrt).then_inc(std_ready, 1)

            def gained_high(row, src, dst, signal, ready, before=0, per_bank=1):
                for d in range(DT):
                    if d % 2 == 0:
                        act.wait_ge(ready, before + per_bank * (d // 2 + 1))
                    act.activation(dst[:, d, :], src(d), ACT.Copy,
                                   scale=gains[:, row * DT + d:row * DT + d + 1]).then_inc(signal, 1)

            def take_gathered(n):
                act.wait_ge(gathered, n)
                for half in range(2):
                    act.activation(xg_hi[:, 4 * half:4 * half + 4, :].rearrange("p d t -> p (d t)"),
                                   banks[GATHER[half]][:], ACT.Copy).then_inc(xg_hi_ready, 1)

            def take_output(signal):
                for half in range(2):
                    act.activation(y_hi[:, half * CW:(half + 1) * CW], banks[OUT[0][half]][:],
                                   ACT.Copy).then_inc(signal, 1)

            def feed_forward(ps, e, ahead=0):
                if ps.moe:
                    warm(ACT.Silu)
                for j, (kind, c, half) in enumerate(FFN_UNITS):
                    if ps.moe and j == 2:
                        act.wait_ge(flag_ready, 1)
                        act.wait_ge(unit_used, ps.units(0, e))
                        take_output(y_hi_ready)
                    for cc in range(NC):
                        if AT[("w1", cc, 1)] + NHI == j:
                            act.wait_ge(unit_used, ps.units(AT[("w1", cc, 1)] + 1, e))
                            if ps.moe or cc:
                                act.wait_ge(hidden_turned, ps.chunks(cc, e))
                            for t in range(ps.tiles):
                                mm = act.activation(hidden[:, t, :], banks[UP1[t]][:], ACT.Silu)
                            mm.then_inc(activated, 1)
                    if ps.moe and j == SCATTER_AT + NHI:
                        act.wait_ge(pick_turned, e + (ps.p0 + 1))
                        act.activation(pick_t[:], banks[PICK_BANK][:, 0:SEQ], ACT.Copy).then_inc(pick_t_ready, 1)
                    for cc in range(NC):
                        if TURN[cc] + NHI == j:
                            act.wait_ge(hidden_turned, ps.chunks(cc + 1, e))
                            for t in range(ps.tiles):
                                dst = hm_hi[:, cc % 2, :] if ps.moe else b_hi[:, cc % 2, t, :]
                                mm = act.activation(dst, turn_bank(ps, cc, t)[:], ACT.Copy)
                            mm.then_inc(hidden_hi, 1)
                    if j >= ahead:
                        split(ps.u0 + j, ps, j, e)
                    if ps.moe and j == 0:
                        take_gathered(e + (ps.p0 + 1))

            act.dma_start(consts[:], table).then_inc(consts_in, 16)
            act.wait_ge(dve_step, 1)
            warm(ACT.Sqrt)
            vector_loads(act, 4, 6)
            norm(0, lambda t: (x_in[t], 16))
            for i in range(NHI - 1):
                split(U_DENSE + i)
            act.dma_start(row_bc[:], bc(b_o[0])).then_inc(bo_in, 16)
            act.dma_start(sink_row[:], bc(attn_sinks[0])).then_inc(misc_in, 16)
            act.dma_start(view3(r_w, DT), router_w[0].rearrange("(k p) e -> p k e", p=P)).then_inc(misc_in, 16)
            norm(1, lambda t: (x_ready, t + 1))
            warm(ACT.Silu)
            gained_high(1, turned_x, a_hi, a_hi_ready, turned)
            split(U_DENSE + NHI - 1)
            feed_forward(PASSES[0], 0, ahead=NHI)

            for i in range(NHI - 1):
                split(U_KV + i)
            norm(2, lambda t: (x_ready, NT + t + 1))
            gained_high(2, kv_x, kv_hi, kv_hi_ready, turned, DT // 2)
            gained_high(3, kv_x, a_hi, a_hi_ready, kv_lo_ready, 0, 2)
            split(U_KV + NHI - 1)
            def add_bias(i):
                n, b, col = ROPE[i]
                if i:
                    act.wait_ge(unit_used, U_KV + 1 + i)
                else:
                    act.wait_ge(kv_done, 1)
                if i >= 2:
                    act.wait_ge(roped, i - 1)
                for k in range(n):
                    mm = act.activation(rope_x[:, i % 2, k, :], banks[b][:, k * SEQ:(k + 1) * SEQ], ACT.Identity,
                                        bias=gains[:, col + k:col + k + 1])
                mm.then_inc(biased, 1)

            for i in range(4):
                add_bias(i)
                if i == 2:
                    warm(ACT.Exp)
                split(U_Q + 2 + i)

            def exponentials(i):
                c, j0, n, nk = STEPS[i]
                act.wait_ge(max_ready, i + 1)
                if i >= 2:
                    act.wait_ge(weighted, i - 1)
                    act.wait_ge(probs_turned, i - 1)
                for a in range(n):
                    keys = slice(a * nk, (a + 1) * nk)
                    act.activation(probs[:, i % 2, keys], banks[i % 2][:, keys], ACT.Exp,
                                   bias=stat(neg_max, i)[:, a:a + 1], scale=HD ** -0.5,
                                   accum_out=stat(sums, i)[:, a:a + 1])
                act.activation(stat(sink_exp, i), stat(sink_in, i), ACT.Exp).then_inc(exped, 1)

            def take_probs(i):
                act.wait_ge(probs_turned, i + 1)
                if i >= 2:
                    act.wait_ge(attended, i - 1)
                act.activation(probs_t[:, i % 2, :], banks[2 + i % 2][:], ACT.Copy).then_inc(probs_out, 1)

            def take_attended(b):
                act.activation(ot_hi[:, 2 * b:2 * b + 2, :].rearrange("p d t -> p (d t)"), banks[4 + b][:],
                               ACT.Copy).then_inc(ot_hi_ready, 1)

            for i in range(NS + 1):
                if i < NS:
                    exponentials(i)
                if i == 1:
                    add_bias(4)
                if i >= 1:
                    take_probs(i - 1)
                if i == 1:
                    split(U_O + 2)
            act.wait_ge(attended, 4)
            take_attended(0)
            take_attended(1)
            act.wait_ge(attended, NS)
            take_attended(2)
            take_attended(3)
            split(U_O + 3)

            norm(3, lambda t: (x_ready, 2 * NT + t + 1))
            warm(ACT.Exp)
            for b in range(4):
                act.wait_ge(turned, (DT // 2) * 2 + b + 1)
                act.activation(h_t[:, 2 * b:2 * b + 2, :].rearrange("p d t -> p (d t)"), banks[4 + b][:],
                               ACT.Copy).then_inc(h_out, 1)
            for t in range(NT):
                act.wait_ge(gained, t + 1)
                act.activation(xs_hi[:, t, :], xn[:, t, :], ACT.Copy).then_inc(xs_hi_ready, 1)
            act.wait_ge(gate_in, 1)
            act.activation(gate_w[:, 2:4], gate_w[:, 0:2], ACT.Exp).then_inc(gate_exp, 1)

            def expert_pass(ps):
                with act.Fori(0, E) as e:
                    feed_forward(ps, e)
                act.wait_ge(unit_used, ps.u0 + E * NU)

            expert_pass(PASSES[1])
            again = act.value_load(over_flag[0:1, 0:1], min_val=0, max_val=1)
            with act.If(again > 0):
                expert_pass(PASSES[2])
            take_output(last_hi)

            norm(4, lambda t: (stream_done, t + 1), dump=squares)

        @block.vector
        def _(dve):
            steps = [0]

            def step(instruction):
                steps[0] += 1
                instruction.then_inc(dve_step, 1)
                dve.wait_ge(dve_step, steps[0])

            def split(u, ps=None, j=0, e=0):
                dve.wait_ge(split_hi, ps.units(j - U_DENSE + 1, e) if ps else u - U_DENSE + 1)
                dve.tensor_tensor(low[slot(u)][:], raw[slot(u)][:], high[hslot(u)][:].bitcast(F32),
                                  ALU.subtract).then_inc(split_lo, 1)

            def norm(n, t):
                c = slice(t, t + 1)
                dve.wait_ge(sumsq_ready, NT * n + t + 1)
                dve.tensor_scalar(var[:, c], sumsq[:, c], 1.0 / D, EPS, ALU.mult, ALU.add).then_inc(var_ready, 1)
                dve.wait_ge(std_ready, NT * n + t + 1)
                step(dve.reciprocal(rstd[:, c], std[:, c]))

            def normalise(n, t):
                norm(n, t)
                dve.tensor_scalar(xn[:, t, :], x_res[:, t, :], rstd[:, t:t + 1], None, ALU.mult).then_inc(xn_ready, 1)

            def normalise_gained(n, t, signal):
                norm(n, t)
                dve.scalar_tensor_tensor(xn[:, t, :], x_res[:, t, :], rstd[:, t:t + 1], row_bc[:],
                                         ALU.mult, ALU.mult).then_inc(signal, 1)

            def update(t, pair):
                for half in range(2):
                    s = slice(half * CW, (half + 1) * CW)
                    mm = dve.tensor_tensor(x_res[:, t, s], x_res[:, t, s], banks[pair[half]][:], ALU.add)
                mm.then_inc(x_ready, 1)

            def gained_low(row, src, hi, lo, ready, before, signal):
                for d in range(DT):
                    if d % 2 == 0:
                        dve.wait_ge(ready, before + d + 2)
                    dve.scalar_tensor_tensor(lo[:, d, :], src(d),
                                             gains[:, row * DT + d:row * DT + d + 1], hi[:, d, :].bitcast(F32),
                                             ALU.mult, ALU.subtract).then_inc(signal, 1)

            def take_gathered(n):
                for half in range(2):
                    dve.wait_ge(xg_hi_ready, n + (half + 1))
                    s = slice(4 * half, 4 * half + 4)
                    mm = dve.tensor_tensor(xg_lo[:, s, :].rearrange("p d t -> p (d t)"), banks[GATHER[half]][:],
                                           xg_hi[:, s, :].bitcast(F32).rearrange("p d t -> p (d t)"), ALU.subtract)
                mm.then_inc(xg_lo_ready, 1)

            def take_output(n, ready, signal):
                for half in range(2):
                    dve.wait_ge(ready, n + (half + 1))
                    s = slice(half * CW, (half + 1) * CW)
                    mm = dve.tensor_tensor(y_lo[:, s], banks[OUT[0][half]][:], y_hi[:, s].bitcast(F32), ALU.subtract)
                mm.then_inc(signal, 1)

            def pick_tokens(ps, expert, before):
                for t in range(NT):
                    mm = dve.tensor_scalar(pick[:, t, :], consts[:, C_IOTA:C_IOTA + P],
                                           pos4[:, ps.block, t, expert], None, ALU.is_equal)
                mm.then_inc(picked, 1)

            def add_scattered(block, column, n, ready, signal):
                for t, pair in enumerate((OUT[0], GATHER)):
                    dve.wait_ge(ready, n + (t + 1))
                    for half in range(2):
                        s = slice(half * CW, (half + 1) * CW)
                        mm = dve.scalar_tensor_tensor(x_res[:, t, s], banks[pair[half]][:], comb4[:, block, t, column],
                                                      x_res[:, t, s], ALU.mult, ALU.add)
                    mm.then_inc(signal, 1)

            def feed_forward(ps, e, ahead=0):
                for j, (kind, c, half) in enumerate(FFN_UNITS):
                    if ps.moe and j == 2:
                        take_output(e * 2 + 2 * ps.p0, y_hi_ready, y_lo_ready)
                    for cc in range(NC):
                        if AT[("w3", cc, 1)] + NHI == j:
                            dve.wait_ge(unit_used, ps.units(AT[("w3", cc, 1)] + 1, e))
                            dve.wait_ge(activated, ps.chunks(cc + 1, e))
                            for t in range(ps.tiles):
                                mm = dve.tensor_tensor(hidden[:, t, :], hidden[:, t, :], banks[UP3[t]][:], ALU.mult)
                            mm.then_inc(gated, 1)
                    if ps.moe and j == SCATTER_AT + NHI:
                        if ps.p0:
                            dve.wait_ge(added, e * 2 + 2 * ps.p0)
                        add_scattered(ps.block, bass.ds(e, 1), e * 2 + 2 * ps.p0, scattered, added)
                    for cc in range(NC):
                        if TURN[cc] + NHI == j:
                            dve.wait_ge(hidden_hi, ps.chunks(cc + 1, e))
                            for t in range(ps.tiles):
                                hi = hm_hi[:, cc % 2, :] if ps.moe else b_hi[:, cc % 2, t, :]
                                lo = hm_lo[:, cc % 2, :] if ps.moe else b_lo[:, cc % 2, t, :]
                                mm = dve.tensor_tensor(lo, turn_bank(ps, cc, t)[:],
                                                       hi.bitcast(F32), ALU.subtract)
                            mm.then_inc(hidden_lo, 1)
                    if ps.moe and j == PICK_AT:
                        dve.wait_ge(pick_turned, e + (ps.p0 + 1))
                        pick_tokens(ps, bass.ds(e + 1, 1), e)
                    if j >= ahead:
                        split(ps.u0 + j, ps, j, e)
                    if ps.moe and j == 0:
                        take_gathered(e * 2 + 2 * ps.p0)

            step(dve.memset(warm_in, 1.0))
            step(dve.memset(position[:], -1.0))
            step(dve.memset(combine[:], 0.0))
            for t in range(NT):
                dve.wait_ge(x_in[t], 16)
                normalise(0, t)
            dve.wait_ge(vec_turned, 1)
            step(dve.tensor_copy(gains[:], banks[7][:, 0:NV]))
            dve.wait_ge(consts_in, 16)
            dve.tensor_scalar(first_key, consts[:, C_IOTA:C_IOTA + E], -1.0, float(E), ALU.mult,
                              ALU.add).then_inc(gains_ready, 1)
            for b in range(4):
                dve.wait_ge(pooled, b + 1)
                for d in (2 * b, 2 * b + 1):
                    mm = dve.tensor_scalar(pooled_t[:, d, :], banks[b][:, (d % 2) * SEQ:(d % 2 + 1) * SEQ],
                                           gains[:, d:d + 1], None, ALU.mult)
                mm.then_inc(pooled_out, 1)
                if b in (1, 2):
                    dve.wait_ge(landed[U_POOLW], 16)
                    dve.wait_ge(pool_in, 32)
                    groups = slice(2 * (b - 1), 2 * b)
                    w = raw[U_POOLW][:].rearrange("p (g k f) -> p g k f", g=4, k=2)[:, groups]
                    scale = pool_rows[:, 1, :].rearrange("p (g f) -> p g f", g=4)[:, groups]
                    dve.tensor_tensor(w, w, scale.unsqueeze(2).to_broadcast([P, 2, 2, SEQ]),
                                      ALU.mult).then_inc(pool_scaled, 1)
            split(U_DENSE)
            for t in range(NT):
                dve.wait_ge(pool_ready, t + 1)
                dve.wait_ge(mixed, t + 1)
                update(t, OUT[t])
            for t in range(NT):
                dve.wait_ge(x_ready, t + 1)
                normalise(1, t)

            split(U_DENSE + 1)
            gained_low(1, turned_x, a_hi, a_lo, a_hi_ready, 0, a_lo_ready)
            split(U_DENSE + NHI - 1)
            feed_forward(PASSES[0], 0, ahead=NHI)
            for i in range(NHI - 1):
                split(U_KV + i)

            for t in range(NT):
                if t < NT - 1:
                    dve.wait_ge(dense_out, t + 1)
                else:
                    dve.wait_ge(unit_used, U_KV)
                update(t, OUT[t])
            for t in range(NT):
                dve.wait_ge(x_ready, NT + t + 1)
                normalise(2, t)
            gained_low(2, kv_x, kv_hi, kv_lo, kv_hi_ready, 0, kv_lo_ready)
            gained_low(3, kv_x, a_hi, a_lo, a_hi_ready, DT, a_lo_ready)
            split(U_KV + NHI - 1)
            sin = consts[:, C_SIN:C_SIN + SEQ]
            half_d = HD // 2

            def rotate(i):
                n, b, _ = ROPE[i]
                dve.wait_ge(biased, i + 1)
                for r in range(0, P, half_d):
                    to = r ^ half_d
                    mm = dve.tensor_tensor(rope_z[to:to + half_d, 0:n, :], rope_x[r:r + half_d, i % 2, 0:n, :],
                                           sin[r:r + half_d].unsqueeze(1).to_broadcast([half_d, n, SEQ]), ALU.mult)
                step(mm)
                dve.wait_ge(cosined, i + 1)
                if i:
                    def by_chunk(t_):
                        return t_.rearrange("p a (c t) -> p a c t", t=CHUNK)

                    dve.tensor_tensor(q_t[:, i - 1, :, :].rearrange("p c (a t) -> p a c t", a=2), by_chunk(rope_y[:]),
                                      by_chunk(rope_z[:]), ALU.add).then_inc(roped, 1)
                else:
                    for g in range(2):
                        for to in (0, HD):
                            s = slice(g * HD, (g + 1) * HD)
                            mm = dve.tensor_tensor(k_t[to:to + HD, g, :], rope_y[s, 0, :], rope_z[s, 0, :], ALU.add)
                    mm.then_inc(roped, 1)
                dve.wait_ge(roped, i + 1)

            rotate(0)
            dve.wait_ge(bv_in, 16)
            dve.wait_ge(unit_used, U_KV + 1)
            for to, c, of, t in ((0, 1, 0, 0), (64, 1, 64, 0), (0, 2, 64, 0), (64, 2, 0, 1), (0, 3, 0, 1),
                                 (64, 3, 64, 1), (0, 0, 0, 0), (64, 0, 0, 0)):
                mm = dve.tensor_tensor(v_win[to:to + CHUNK, c, :], banks[5][of:of + CHUNK, t * P:(t + 1) * P],
                                       b_v[of:of + CHUNK, :], ALU.add)
            mm.then_inc(v_out, 1)
            split(U_Q + 2)
            rotate(1)
            split(U_Q + 3)
            dve.wait_ge(misc_in, 16 * 2)
            for a in range(2):
                rows = slice(a * CHUNK, (a + 1) * CHUNK)
                mm = dve.tensor_copy(sinks[rows, :].rearrange("p (g r b) -> p g r b", g=2, r=2),
                                     sink_row[rows, :].rearrange("p (g b a r) -> p a g r b", g=2, a=2, b=2)[:, a])
            step(mm)
            step(dve.tensor_scalar(neg_sinks[:], sinks[:], -1.0, None, ALU.mult))
            rotate(2)
            rotate(3)

            def maxima_of(i):
                c, j0, n, nk = STEPS[i]
                dve.wait_ge(scored, i + 1)
                if i >= 2:
                    dve.wait_ge(exped, i - 1)
                step(dve.tensor_reduce(stat(maxima, i), banks[i % 2][:].rearrange("p (h k) -> p h k", h=n), AX_X,
                                       ALU.max))
                step(dve.scalar_tensor_tensor(stat(neg_max, i), stat(maxima, i), -(HD ** -0.5),
                                              neg_sinks[:, j0:j0 + n], ALU.mult, ALU.min))
                dve.tensor_tensor(stat(sink_in, i), sinks[:, j0:j0 + n], stat(neg_max, i),
                                  ALU.add).then_inc(max_ready, 1)

            def weigh(i):
                c, j0, n, nk = STEPS[i]
                dve.wait_ge(exped, i + 1)
                step(dve.tensor_tensor(denom[:, 0:n], stat(sums, i), stat(sink_exp, i), ALU.add))
                step(dve.reciprocal(stat(recip, i), denom[:, 0:n]))
                sc = probs[:, i % 2, :].rearrange("p (h k) -> p h k", h=n)
                dve.tensor_tensor(sc, sc, stat(recip, i).unsqueeze(2).to_broadcast([P, n, nk]),
                                  ALU.mult).then_inc(weighted, 1)

            for i in range(NS + 1):
                if i < NS:
                    maxima_of(i)
                if i == 1:
                    split(U_O)
                if i >= 1:
                    weigh(i - 1)
                if i == 1:
                    rotate(4)
                if i in O_SPLITS:
                    split(U_O + O_SPLITS[i])
            for b in range(4):
                dve.wait_ge(ot_hi_ready, b + 1)
                dve.tensor_tensor(ot_lo[:, 2 * b:2 * b + 2, :].rearrange("p d t -> p (d t)"), banks[4 + b][:],
                                  ot_hi[:, 2 * b:2 * b + 2, :].bitcast(F32).rearrange("p d t -> p (d t)"),
                                  ALU.subtract).then_inc(ot_lo_ready, 1)
            split(U_O + 3)

            dve.wait_ge(bo_added, NT)
            dve.wait_ge(gn_in, 16)
            for t in range(NT):
                if t < NT - 1:
                    dve.wait_ge(proj_out, t + 1)
                else:
                    dve.wait_ge(unit_used, U_O + 4)
                update(t, PROJ[t])
            for t in range(NT):
                dve.wait_ge(x_ready, 2 * NT + t + 1)
                normalise_gained(3, t, gained)
            dve.wait_ge(gained, NT)
            for t in range(NT):
                dve.wait_ge(xs_hi_ready, t + 1)
                dve.tensor_tensor(xs_lo[:, t, :], xn[:, t, :], xs_hi[:, t, :].bitcast(F32),
                                  ALU.subtract).then_inc(xs_lo_ready, 1)
            dve.wait_ge(routed, 1)
            for t in range(NT):
                mm = dve.tensor_copy(logits[:, t * E:(t + 1) * E], banks[LOGITS[t]][:, 0:E])
            step(mm)
            for t in range(NT):
                step(dve.max(top[:, t * 8:t * 8 + 8], logits[:, t * E:(t + 1) * E]))
            tops = view3(top, NT)
            dve.tensor_tensor(gate_w[:, 0:2], tops[:, :, 1], tops[:, :, 0], ALU.subtract).then_inc(gate_in, 1)
            def per_tile(column):
                return column.unsqueeze(2).to_broadcast([P, NT, E])

            keys = first_key.unsqueeze(1).to_broadcast([P, NT, E])
            eq3, run3 = view3(eq, NT), view3(run, NT)
            for rank, (of, to) in enumerate(((logits, first), (rest, second))):
                step(dve.tensor_tensor(eq3, view3(of, NT), per_tile(tops[:, :, rank]), ALU.is_equal))
                step(dve.tensor_tensor(run3, eq3, keys, ALU.mult))
                step(dve.tensor_reduce(best, run3, AX_X, ALU.max))
                step(dve.tensor_tensor(view3(to, NT), run3, per_tile(best), ALU.is_equal))
                if rank == 0:
                    step(dve.scalar_tensor_tensor(rest[:], first[:], -3e38, logits[:], ALU.mult, ALU.add))
            dve.tensor_tensor(chosen[:], first[:], second[:], ALU.add).then_inc(chosen_ready, 1)
            dve.wait_ge(counted, 1)
            step(dve.tensor_tensor(run[:], banks[5][:, 0:NT * E], chosen[:], ALU.mult))
            step(dve.tensor_scalar(pos4[:, 0, :, 0:E], run3, -1.0, None, ALU.add))

            def finish_routing():
                step(dve.tensor_scalar(pos4[:, 1, :, :], pos4[:, 0, :, :], -float(P), None, ALU.add))
                step(dve.tensor_reduce(over[:, 0:1], banks[5][:, 2 * E:3 * E], AX_X, ALU.max))
                dve.tensor_scalar(over_flag[:], over[:, 0:1], float(P), None, ALU.is_gt).then_inc(flag_ready, 1)
                dve.wait_ge(gate_exp, 1)
                step(dve.tensor_scalar(gate_w[:, 0:2], gate_w[:, 2:4], 1.0, None, ALU.add))
                step(dve.reciprocal(gate_w[:, 0:2], gate_w[:, 0:2]))
                step(dve.tensor_tensor(gate_w[:, 2:4], gate_w[:, 2:4], gate_w[:, 0:2], ALU.mult))
                step(dve.tensor_tensor(run3, view3(second, NT), per_tile(gate_w[:, 2:4]), ALU.mult))
                step(dve.tensor_tensor(eq3, view3(first, NT), per_tile(gate_w[:, 0:2]), ALU.mult))
                for block in range(2):
                    mm = dve.tensor_tensor(comb4[:, block, :, 1:E + 1], eq3, run3, ALU.add)
                step(mm)
                step(dve.tensor_copy(comb4[:, 1, :, 0:1], comb4[:, 0, :, E:E + 1]))

            def expert_pass(ps):
                if ps.p0:
                    dve.wait_ge(pick_turned, ps.p0)
                    dve.wait_ge(gathered, ps.p0)
                pick_tokens(ps, slice(0, 1), 0)
                if not ps.p0:
                    finish_routing()
                with dve.Fori(0, E) as e:
                    feed_forward(ps, e)
                dve.wait_ge(added, 2 * (ps.p0 + E))

            expert_pass(PASSES[1])
            dve.wait_ge(flag_ready, 1)
            again = dve.value_load(over_flag[0:1, 0:1], min_val=0, max_val=1)
            with dve.If(again > 0):
                expert_pass(PASSES[2])

            take_output(0, last_hi, last_lo)
            add_scattered(0, slice(E, E + 1), 0, last_scattered, stream_done)
            dve.wait_ge(gf_in, 16)
            for t in range(NT):
                dve.wait_ge(stream_done, t + 1)
                normalise_gained(4, t, xn_ready)


_INS = ["x", "norm_mix", "norm_ffn", "pool_w", "pool_b", "pool_scale", "norm_kv", "w_kv", "b_kv", "w_q", "b_q",
        "attn_sinks", "w_o", "b_o", "ffn_w1", "ffn_w3", "ffn_w2", "router_w", "moe_w1", "moe_w3", "moe_w2",
        "norm_final"]


def kernel(**inputs):
    import concourse.bacc as bacc
    from concourse.bass_utils import run_bass_kernel_spmd

    table, bands = shape_constants()
    nc = bacc.Bacc("TRN2", target_bir_lowering=False, num_devices=1)
    arrays = {f"in_{name}": np.ascontiguousarray(inputs[name]) for name in _INS}
    arrays["in_table"] = table
    arrays["in_bands"] = bands
    args = [nc.dram_tensor(name, a.shape, mybir.dt.from_np(a.dtype), kind="ExternalInput").ap()
            for name, a in arrays.items()]
    out = nc.dram_tensor("out_x", (1, SEQ, D), F32, kind="ExternalOutput").ap()
    trunk_program(nc, *args, out)
    result = run_bass_kernel_spmd(nc, [arrays], core_ids=[0])
    return result.results[0]["out_x"]
```
